# Optimizing a Trainium2 kernel written in Bass

```python
import math
import jax, jax.numpy as jnp
from jax import lax
import numpy as np
import jax
import jax.numpy as jnp

D_MODEL = 2048
BATCH = 1
SEQ = 256
DEPTH = 2

D_MIX = D_MODEL
A_HEADS = 4
A_HEAD_DIM = 128
A_QK_HALF = A_HEAD_DIM // 2
D_A = A_HEADS * A_HEAD_DIM
B_HEADS = 8
B_HEAD_DIM = 128
D_B = B_HEADS * B_HEAD_DIM
DILATED_PATTERNS = ((128, 1), (512, 4), (2048, 16))
D_C = D_MIX - D_A - D_B
CONV_WIDTH = 31

BLOCK = 128
N_BUCKETS = 32
MAX_DISTANCE = 2048
N_ATTN_HEADS = A_HEADS + B_HEADS
ALPHA = (2 * DEPTH) ** 0.25
BETA = (8 * DEPTH) ** -0.25
EPS = 1e-5

IN_SIZES = (D_A, D_A, D_A, D_A,
            D_B, D_B, D_B, D_B,
            D_C, D_C, D_C)
D_IN = sum(IN_SIZES)
IN_OFFSETS = [int(o) for o in np.cumsum(IN_SIZES)[:-1]]


def layer_norm(x, g, b):
    x32 = x.astype(jnp.float32)
    mu = jnp.mean(x32, axis=-1, keepdims=True)
    var = jnp.mean(jnp.square(x32 - mu), axis=-1, keepdims=True)
    y = (x32 - mu) * lax.rsqrt(var + EPS) * g.astype(jnp.float32) + b.astype(jnp.float32)
    return y.astype(x.dtype)

def t5_bucket(dist):
    max_exact = N_BUCKETS // 2
    d = jnp.maximum(dist, 0)
    df = jnp.maximum(d, 1).astype(jnp.float32)
    large = max_exact + (jnp.log(df / max_exact) / math.log(MAX_DISTANCE / max_exact)
                         * (N_BUCKETS - max_exact)).astype(jnp.int32)
    large = jnp.minimum(large, N_BUCKETS - 1)
    return jnp.where(d < max_exact, d, large)

def diff_attention(q, k, v, bias_dist, lam, lam_init, head_gain):
    B, S, H, _, Dq = q.shape
    nb = S // BLOCK
    scale = Dq ** -0.5
    qb = jnp.moveaxis(q.reshape(B, nb, BLOCK, H, 2, Dq), 1, 0)
    k_pos = jnp.arange(S)

    def one_block(args):
        qi, i = args
        q_pos = i * BLOCK + jnp.arange(BLOCK)
        dist = q_pos[:, None] - k_pos[None, :]
        bias = bias_dist[jnp.clip(dist, 0, S - 1)].astype(jnp.float32)
        s = jnp.einsum('bqhcd,bkhcd->bhcqk', qi, k).astype(jnp.float32) * scale
        s = s + jnp.transpose(bias, (2, 0, 1))[None, :, None]
        s = jnp.where(dist >= 0, s, -jnp.inf)
        p = jax.nn.softmax(s, axis=-1)
        a = p[:, :, 0] - lam * p[:, :, 1]
        return jnp.einsum('bhqk,bkhd->bqhd', a.astype(v.dtype), v)

    out = lax.map(one_block, (qb, jnp.arange(nb)))
    out = jnp.moveaxis(out, 0, 1).reshape(B, S, H, v.shape[-1]).astype(jnp.float32)
    out = out * lax.rsqrt(jnp.mean(jnp.square(out), axis=-1, keepdims=True) + EPS)
    out = out * head_gain.astype(jnp.float32) * (1.0 - lam_init)
    return out.astype(v.dtype)

def _residue_view(x, dil):
    B, S = x.shape[:2]
    L = S // dil
    xr = jnp.moveaxis(x.reshape((B, L, dil) + x.shape[2:]), 2, 1).reshape((B * dil, L) + x.shape[2:])
    pad = (-L) % BLOCK
    return jnp.pad(xr, ((0, 0), (0, pad)) + ((0, 0),) * (x.ndim - 2))

def _residue_unview(y, B, dil, L):
    y = y[:, :L]
    y = jnp.moveaxis(y.reshape((B, dil) + y.shape[1:]), 1, 2)
    return y.reshape((B, dil * L) + y.shape[3:])

def dilated_attention(q, k, v, bias_table):
    B, S, H, D = q.shape
    scale = D ** -0.5
    qi = jnp.arange(BLOCK)
    kj = jnp.arange(2 * BLOCK)
    lag = BLOCK + qi[:, None] - kj[None, :]
    outs, maxes, sums = [], [], []
    for window, dil in DILATED_PATTERNS:
        L = S // dil
        qr, kr, vr = _residue_view(q, dil), _residue_view(k, dil), _residue_view(v, dil)
        N, Lp = qr.shape[:2]
        nb = Lp // BLOCK
        qb = qr.reshape(N, nb, BLOCK, H, D)
        kp = jnp.pad(kr, ((0, 0), (BLOCK, 0), (0, 0), (0, 0))).reshape(N, nb + 1, BLOCK, H, D)
        vp = jnp.pad(vr, ((0, 0), (BLOCK, 0), (0, 0), (0, 0))).reshape(N, nb + 1, BLOCK, H, D)
        kb = jnp.concatenate([kp[:, :-1], kp[:, 1:]], axis=2)
        vb = jnp.concatenate([vp[:, :-1], vp[:, 1:]], axis=2)
        key_idx = (jnp.arange(nb) * BLOCK - BLOCK)[:, None] + kj[None, :]
        valid = ((lag >= 0) & (lag <= window // dil))[None] & (key_idx >= 0)[:, None, :]
        bias = bias_table[t5_bucket(kj * dil)]
        bias_qk = bias[jnp.clip(lag, 0, 2 * BLOCK - 1)].astype(jnp.float32)
        s = jnp.einsum('nbqhd,nbkhd->nbhqk', qb, kb).astype(jnp.float32) * scale
        s = s + jnp.transpose(bias_qk, (2, 0, 1))[None, None]
        s = jnp.where(valid[None, :, None], s, -jnp.inf)
        m = jnp.max(s, axis=-1)
        p = jnp.exp(s - m[..., None])
        l = jnp.sum(p, axis=-1)
        o = jnp.einsum('nbhqk,nbkhd->nbqhd', p.astype(v.dtype), vb).astype(jnp.float32)
        l_t = jnp.swapaxes(l, 2, 3)
        o = o / l_t[..., None]
        outs.append(_residue_unview(o.reshape(N, Lp, H, D), B, dil, L))
        maxes.append(_residue_unview(jnp.swapaxes(m, 2, 3).reshape(N, Lp, H), B, dil, L))
        sums.append(_residue_unview(l_t.reshape(N, Lp, H), B, dil, L))
    m_all = jnp.stack(maxes)
    w = jnp.stack(sums) * jnp.exp(m_all - jnp.max(m_all, axis=0, keepdims=True))
    out = jnp.sum(w[..., None] * jnp.stack(outs), axis=0) / jnp.sum(w, axis=0)[..., None]
    return out.astype(q.dtype)

def conformer_conv(u, glu_gate, w_dw, b_dw, ln_g, ln_b, w_pw):
    h = u * jax.nn.sigmoid(glu_gate)
    h = lax.conv_general_dilated(h, w_dw[:, None, :], window_strides=(1,),
                                 padding=[(CONV_WIDTH - 1, 0)],
                                 dimension_numbers=('NWC', 'WIO', 'NWC'),
                                 feature_group_count=D_C) + b_dw
    h = jax.nn.silu(layer_norm(h, ln_g, ln_b))
    return h @ w_pw

def hybrid_layer(x, w_in, diff_lambda, diff_head_gain, conv_dw, conv_b, conv_ln_g, conv_ln_b,
                 conv_pw, w_out, ln_g, ln_b, rel_bias, lam_init):
    B, S, _ = x.shape
    proj = x @ w_in
    aq, ak, av, ag, bq, bk, bv, bg, cu, cglu, cg = jnp.split(proj, IN_OFFSETS, axis=-1)

    lam_v = diff_lambda.astype(jnp.float32)
    lam = (jnp.exp(jnp.sum(lam_v[0] * lam_v[1])) - jnp.exp(jnp.sum(lam_v[2] * lam_v[3]))
           + lam_init)
    bias_a = rel_bias[t5_bucket(jnp.arange(S))][:, :A_HEADS]
    ya = diff_attention(aq.reshape(B, S, A_HEADS, 2, A_QK_HALF),
                        ak.reshape(B, S, A_HEADS, 2, A_QK_HALF),
                        av.reshape(B, S, A_HEADS, A_HEAD_DIM),
                        bias_a, lam, lam_init, diff_head_gain).reshape(B, S, D_A)
    ya = ya * jax.nn.silu(ag)

    yb = dilated_attention(bq.reshape(B, S, B_HEADS, B_HEAD_DIM),
                           bk.reshape(B, S, B_HEADS, B_HEAD_DIM),
                           bv.reshape(B, S, B_HEADS, B_HEAD_DIM),
                           rel_bias[:, A_HEADS:]).reshape(B, S, D_B)
    yb = yb * jax.nn.silu(bg)

    yc = conformer_conv(cu, cglu, conv_dw, conv_b, conv_ln_g, conv_ln_b, conv_pw)
    yc = yc * jax.nn.silu(cg)

    y = jnp.concatenate([ya, yb, yc], axis=-1) @ w_out
    return layer_norm(ALPHA * x + y, ln_g, ln_b)

def first_inputs(seed: int = 0) -> dict:
    key = jax.random.key(seed)
    ks = jax.random.split(key, 14)
    nrm = jax.random.normal
    return {
        "x": nrm(ks[0], (BATCH, SEQ, D_MODEL), jnp.float32),
        "w_in": nrm(ks[1], (DEPTH, D_MODEL, D_IN), jnp.float32) * D_MODEL ** -0.5,
        "diff_lambda": 0.1 * nrm(ks[2], (DEPTH, 4, A_QK_HALF), jnp.float32),
        "diff_head_gain": 1.0 + 0.02 * nrm(ks[3], (DEPTH, A_HEAD_DIM), jnp.float32),
        "conv_dw": nrm(ks[4], (DEPTH, CONV_WIDTH, D_C), jnp.float32) * CONV_WIDTH ** -0.5,
        "conv_b": 0.02 * nrm(ks[5], (DEPTH, D_C), jnp.float32),
        "conv_ln_g": 1.0 + 0.02 * nrm(ks[6], (DEPTH, D_C), jnp.float32),
        "conv_ln_b": 0.02 * nrm(ks[7], (DEPTH, D_C), jnp.float32),
        "conv_pw": nrm(ks[8], (DEPTH, D_C, D_C), jnp.float32) * D_C ** -0.5,
        "w_out": nrm(ks[9], (DEPTH, D_MIX, D_MODEL), jnp.float32) * (D_MIX ** -0.5 * BETA),
        "ln_g": 1.0 + 0.02 * nrm(ks[10], (DEPTH, D_MODEL), jnp.float32),
        "ln_b": 0.02 * nrm(ks[11], (DEPTH, D_MODEL), jnp.float32),
        "rel_bias": 0.5 * nrm(ks[12], (N_BUCKETS, N_ATTN_HEADS), jnp.float32),
    }

def first_block(x, w_in, diff_lambda, diff_head_gain, conv_dw, conv_b, conv_ln_g, conv_ln_b,
              conv_pw, w_out, ln_g, ln_b, rel_bias):
    for layer in range(DEPTH):
        lam_init = 0.8 - 0.6 * math.exp(-0.3 * layer)
        x = hybrid_layer(x, w_in[layer], diff_lambda[layer], diff_head_gain[layer],
                         conv_dw[layer], conv_b[layer], conv_ln_g[layer], conv_ln_b[layer],
                         conv_pw[layer], w_out[layer], ln_g[layer], ln_b[layer], rel_bias,
                         lam_init)
    return x


DEPTH_2 = 1

GRID_W = 64
CTX_LEN = 256

NA_HEADS = 8
NA_HEAD_DIM = 128
NA_WIDTH = NA_HEADS * NA_HEAD_DIM
NA_KH_MAX = 8
NA_KW = 16

FT_GROUPS = 4
FT_GROUP_DIM = 128
FT_WIDTH = FT_GROUPS * FT_GROUP_DIM

POOL_WINDOWS = (2, 4, 8, 16)
POOL_GROUP_DIM = 128
POOL_WIDTH = len(POOL_WINDOWS) * POOL_GROUP_DIM

SC_WIDTH = 512
SC_CONV = 3

N_BRANCH = 4
IN_WIDTH = 3 * NA_WIDTH + FT_WIDTH + POOL_WIDTH + 3 * SC_WIDTH
D_FF = 256 * math.ceil(8 * D_MODEL / (3 * 256))
N_MOD = 6
RMS_EPS = 1e-6


def rms_norm(x, w):
    xf = x.astype(jnp.float32)
    y = xf * lax.rsqrt(jnp.mean(xf * xf, axis=-1, keepdims=True) + RMS_EPS)
    return (y * w.astype(jnp.float32)).astype(x.dtype)

def modulate(h, shift, scale):
    return h * (1 + scale) + shift

def in_split_points():
    widths = (NA_WIDTH, NA_WIDTH, NA_WIDTH, FT_WIDTH, POOL_WIDTH, SC_WIDTH, SC_WIDTH)
    return [int(s) for s in np.cumsum(widths)]

def mixer_inputs(h, w_in, q_norm_w, k_norm_w):
    b, l, _ = h.shape
    q, k, v, ft, pool, sv, sb, sc = jnp.split(h @ w_in, in_split_points(), axis=-1)
    q = rms_norm(q.reshape(b, l, NA_HEADS, NA_HEAD_DIM), q_norm_w)
    k = rms_norm(k.reshape(b, l, NA_HEADS, NA_HEAD_DIM), k_norm_w)
    v = v.reshape(b, l, NA_HEADS, NA_HEAD_DIM)
    return q, k, v, ft, pool, sv, sb, sc

def context_kv(hc, w_in, k_norm_w):
    b, l, _ = hc.shape
    k = (hc @ w_in[:, NA_WIDTH:2 * NA_WIDTH]).reshape(b, l, NA_HEADS, NA_HEAD_DIM)
    v = (hc @ w_in[:, 2 * NA_WIDTH:3 * NA_WIDTH]).reshape(b, l, NA_HEADS, NA_HEAD_DIM)
    return rms_norm(k, k_norm_w), v

def context_attention(q, k, v):
    s = jnp.einsum('blhd,bmhd->bhlm', q, k, preferred_element_type=jnp.float32) * (NA_HEAD_DIM ** -0.5)
    p = jax.nn.softmax(s, axis=-1).astype(v.dtype)
    o = jnp.einsum('bhlm,bmhd->blhd', p, v)
    return o.reshape(q.shape[0], q.shape[1], NA_WIDTH)

def neighbourhood_attention(q, k, v, k_ctx, v_ctx, rpb):
    b, s, h, dh = q.shape
    rows = s // GRID_W
    kh = min(NA_KH_MAX, rows)
    qg = q.reshape(b, rows, GRID_W, h, dh)
    kg = k.reshape(b, rows, GRID_W, h, dh)
    vg = v.reshape(b, rows, GRID_W, h, dh)
    cols = np.arange(GRID_W)
    col_start = np.clip(cols - NA_KW // 2, 0, GRID_W - NA_KW)
    col_idx = col_start[:, None] + np.arange(NA_KW)[None, :]
    col_off = col_idx - cols[:, None] + (NA_KW - 1)
    bias_cols = jnp.transpose(rpb[:, :, col_off], (0, 2, 1, 3))
    scale = dh ** -0.5

    def row_block(r):
        rs = jnp.clip(r - kh // 2, 0, rows - kh)
        k_win = lax.dynamic_slice_in_dim(kg, rs, kh, axis=1)[:, :, col_idx]
        v_win = lax.dynamic_slice_in_dim(vg, rs, kh, axis=1)[:, :, col_idx]
        q_r = lax.dynamic_index_in_dim(qg, r, axis=1, keepdims=False)
        s_loc = jnp.einsum('bjhd,bajwhd->bhjaw', q_r, k_win, preferred_element_type=jnp.float32) * scale
        row_off = rs + jnp.arange(kh) - r + (NA_KH_MAX - 1)
        s_loc = s_loc + bias_cols[:, :, row_off].astype(jnp.float32)[None]
        s_ctx = jnp.einsum('bjhd,blhd->bhjl', q_r, k_ctx, preferred_element_type=jnp.float32) * scale
        s_all = jnp.concatenate([s_loc.reshape(b, h, GRID_W, kh * NA_KW), s_ctx], axis=-1)
        p = jax.nn.softmax(s_all, axis=-1).astype(v.dtype)
        p_loc = p[..., :kh * NA_KW].reshape(b, h, GRID_W, kh, NA_KW)
        p_ctx = p[..., kh * NA_KW:]
        return jnp.einsum('bhjaw,bajwhd->bjhd', p_loc, v_win) + jnp.einsum('bhjl,blhd->bjhd', p_ctx, v_ctx)

    out = lax.map(row_block, jnp.arange(rows))
    return jnp.transpose(out, (1, 0, 2, 3, 4)).reshape(b, s, h * dh)

def fourier_mix(u):
    b, l, _ = u.shape
    ug = u.astype(jnp.float32).reshape(b, l, FT_GROUPS, FT_GROUP_DIM)
    f = jnp.fft.fft2(ug, axes=(1, 3), norm='ortho').real
    return f.reshape(b, l, FT_WIDTH).astype(u.dtype)

def pool_mix(u, w_pool, pool_scale):
    b, l, _ = u.shape
    uf = u.astype(jnp.float32)
    cs = jnp.pad(jnp.cumsum(uf, axis=1), ((0, 0), (1, 0), (0, 0)))
    pos = jnp.arange(l)
    outs = []
    for g, w in enumerate(POOL_WINDOWS):
        lo = jnp.clip(pos - w // 2, 0, l)
        hi = jnp.clip(pos - w // 2 + w, 0, l)
        c0, c1 = g * POOL_GROUP_DIM, (g + 1) * POOL_GROUP_DIM
        win_sum = cs[:, hi, c0:c1] - cs[:, lo, c0:c1]
        cnt = (hi - lo).astype(jnp.float32)[None, :, None]
        outs.append(win_sum / cnt - uf[:, :, c0:c1])
    p = jnp.stack(outs, axis=2)
    y = jnp.einsum('blgc,gcd->blgd', p, w_pool.astype(jnp.float32)).reshape(b, l, POOL_WIDTH)
    return (y * pool_scale.astype(jnp.float32)).astype(u.dtype)

def short_conv_mix(sv, sb, sc, conv_w):
    u = sc * sv
    up = jnp.pad(u, ((0, 0), (1, 1), (0, 0)))
    y = up[:, :-2] * conv_w[0] + up[:, 1:-1] * conv_w[1] + up[:, 2:] * conv_w[2]
    return sb * y

def merge_branches(h, branches, w_gate, w_branch, w_o):
    y = jax.nn.sigmoid(h @ w_gate[0]) * (branches[0] @ w_branch[0])
    for i in range(1, N_BRANCH):
        y = y + jax.nn.sigmoid(h @ w_gate[i]) * (branches[i] @ w_branch[i])
    return y @ w_o

def swiglu(h, w_g, w_u, w_d):
    return (jax.nn.silu(h @ w_g) * (h @ w_u)) @ w_d

def second_inputs(seed: int = 0) -> dict:
    key = jax.random.key(seed)
    ks = jax.random.split(key, 32)
    f32 = jnp.float32
    L = DEPTH_2
    D = D_MODEL

    def nrm(k, shape, scale):
        return jax.random.normal(k, shape, f32) * scale

    return {
        'x': nrm(ks[0], (BATCH, SEQ, D), 1.0),
        'c': nrm(ks[1], (BATCH, D), 1.0),
        'ctx': nrm(ks[2], (BATCH, CTX_LEN, D), 1.0),
        'c_ctx': nrm(ks[3], (D,), 1.0),
        'w_mod': nrm(ks[4], (L, D, N_MOD * D), D ** -0.5),
        'b_mod': nrm(ks[5], (L, N_MOD * D), 0.01),
        'norm1_w': 1.0 + nrm(ks[6], (L, D), 0.05),
        'w_in': nrm(ks[7], (L, D, IN_WIDTH), D ** -0.5),
        'q_norm_w': 1.0 + nrm(ks[8], (L, NA_HEAD_DIM), 0.05),
        'k_norm_w': 1.0 + nrm(ks[9], (L, NA_HEAD_DIM), 0.05),
        'rpb': nrm(ks[10], (L, NA_HEADS, 2 * NA_KH_MAX - 1, 2 * NA_KW - 1), 0.5),
        'w_pool': nrm(ks[11], (L, len(POOL_WINDOWS), POOL_GROUP_DIM, POOL_GROUP_DIM), POOL_GROUP_DIM ** -0.5),
        'pool_scale': 1.0 + nrm(ks[12], (L, POOL_WIDTH), 0.05),
        'conv_w': nrm(ks[13], (L, SC_CONV, SC_WIDTH), SC_CONV ** -0.5),
        'w_gate': nrm(ks[14], (L, N_BRANCH, D, D), D ** -0.5),
        'w_pa': nrm(ks[15], (L, NA_WIDTH, D), NA_WIDTH ** -0.5),
        'w_pb': nrm(ks[16], (L, FT_WIDTH, D), FT_WIDTH ** -0.5),
        'w_pc': nrm(ks[17], (L, POOL_WIDTH, D), POOL_WIDTH ** -0.5),
        'w_pd': nrm(ks[18], (L, SC_WIDTH, D), SC_WIDTH ** -0.5),
        'w_o': nrm(ks[19], (L, D, D), D ** -0.5),
        'norm2_w': 1.0 + nrm(ks[20], (L, D), 0.05),
        'w_ffn_gate': nrm(ks[21], (L, D, D_FF), D ** -0.5),
        'w_ffn_up': nrm(ks[22], (L, D, D_FF), D ** -0.5),
        'w_ffn_down': nrm(ks[23], (L, D_FF, D), D_FF ** -0.5),
    }

def second_block(x, c, ctx, c_ctx, w_mod, b_mod, norm1_w, w_in, q_norm_w, k_norm_w, rpb, w_pool,
              pool_scale, conv_w, w_gate, w_pa, w_pb, w_pc, w_pd, w_o, norm2_w, w_ffn_gate,
              w_ffn_up, w_ffn_down):
    xc = ctx
    for i in range(DEPTH_2):
        w_branch = (w_pa[i], w_pb[i], w_pc[i], w_pd[i])
        mod = jnp.split(jax.nn.silu(c) @ w_mod[i] + b_mod[i], N_MOD, axis=-1)
        sh1, sc1, g1, sh2, sc2, g2 = [m[:, None, :] for m in mod]
        csh1, csc1, cg1, csh2, csc2, cg2 = jnp.split(jax.nn.silu(c_ctx) @ w_mod[i] + b_mod[i], N_MOD, axis=-1)

        hc = modulate(rms_norm(xc, norm1_w[i]), csh1, csc1)
        if i == DEPTH_2 - 1:
            kc, vc = context_kv(hc, w_in[i], k_norm_w[i])
        else:
            qc, kc, vc, ftc, poolc, svc, sbc, scc = mixer_inputs(hc, w_in[i], q_norm_w[i], k_norm_w[i])
            branches_c = (context_attention(qc, kc, vc), fourier_mix(ftc),
                          pool_mix(poolc, w_pool[i], pool_scale[i]), short_conv_mix(svc, sbc, scc, conv_w[i]))
            xc = xc + cg1 * merge_branches(hc, branches_c, w_gate[i], w_branch, w_o[i])
            xc = xc + cg2 * swiglu(modulate(rms_norm(xc, norm2_w[i]), csh2, csc2),
                                   w_ffn_gate[i], w_ffn_up[i], w_ffn_down[i])

        h = modulate(rms_norm(x, norm1_w[i]), sh1, sc1)
        q, k, v, ft, pool, sv, sb, sc = mixer_inputs(h, w_in[i], q_norm_w[i], k_norm_w[i])
        branches = (neighbourhood_attention(q, k, v, kc, vc, rpb[i]), fourier_mix(ft),
                    pool_mix(pool, w_pool[i], pool_scale[i]), short_conv_mix(sv, sb, sc, conv_w[i]))
        x = x + g1 * merge_branches(h, branches, w_gate[i], w_branch, w_o[i])
        x = x + g2 * swiglu(modulate(rms_norm(x, norm2_w[i]), sh2, sc2),
                            w_ffn_gate[i], w_ffn_up[i], w_ffn_down[i])
    return x


def setup_inputs(seed=0):
    out = dict(first_inputs(seed))
    for name, value in second_inputs(seed + 1).items():
        if name != "x":
            out[name + "_2"] = value
    return out


def reference(
    x, w_in, diff_lambda, diff_head_gain, conv_dw, conv_b, conv_ln_g, conv_ln_b, conv_pw, w_out,
    ln_g, ln_b, rel_bias, c_2, ctx_2, c_ctx_2, w_mod_2, b_mod_2, norm1_w_2, w_in_2, q_norm_w_2,
    k_norm_w_2, rpb_2, w_pool_2, pool_scale_2, conv_w_2, w_gate_2, w_pa_2, w_pb_2, w_pc_2,
    w_pd_2, w_o_2, norm2_w_2, w_ffn_gate_2, w_ffn_up_2, w_ffn_down_2,
):
    x = first_block(
        x, w_in, diff_lambda, diff_head_gain, conv_dw, conv_b, conv_ln_g, conv_ln_b, conv_pw,
        w_out, ln_g, ln_b, rel_bias,
    )
    return second_block(
        x, c_2, ctx_2, c_ctx_2, w_mod_2, b_mod_2, norm1_w_2, w_in_2, q_norm_w_2, k_norm_w_2,
        rpb_2, w_pool_2, pool_scale_2, conv_w_2, w_gate_2, w_pa_2, w_pb_2, w_pc_2, w_pd_2,
        w_o_2, norm2_w_2, w_ffn_gate_2, w_ffn_up_2, w_ffn_down_2,
    )


_drawn_inputs = setup_inputs


def setup_inputs(seed=0):
    import zlib

    import numpy as np

    out = dict(_drawn_inputs(seed))
    spreads = {}
    factors = {'diff_head_gain': 8.0,
     'conv_b': 8.0,
     'conv_ln_g': 8.0,
     'conv_ln_b': 8.0,
     'ctx_2': 2.726,
     'b_mod_2': 2.909,
     'q_norm_w_2': 8.0,
     'k_norm_w_2': 8.0,
     'rpb_2': 7.121,
     'pool_scale_2': 3.957,
     'norm2_w_2': 2.918}
    for name, (base, spread) in spreads.items():
        noise = np.random.default_rng([zlib.crc32(name.encode()), seed]).standard_normal(out[name].shape)
        drawn = base * np.exp(spread * noise) if base else spread * noise
        out[name] = jnp.asarray(drawn.astype(out[name].dtype))
    for name, factor in factors.items():
        out[name] = (out[name] * factor).astype(out[name].dtype)
    return out
```

```python
import math
from contextlib import ExitStack, contextmanager

import numpy as np

import concourse.bass as bass
from concourse import mybir

F32 = mybir.dt.float32
F32R = mybir.dt.float32r
ALU = mybir.AluOpType
ACT = mybir.ActivationFunctionType
AX_X = mybir.AxisListType.X

P = 128
D = 2048
S = 256
TT = S // P
KT = D // P
COLS = 512
DEPTH = 2
A_HEADS, B_HEADS, NA_HEADS = 4, 8, 8
HD = 128
D_A, D_B, D_C = A_HEADS * HD, B_HEADS * HD, 512
CONV = 31
N_BUCKETS, MAX_DISTANCE = 32, 2048
ALPHA = (2 * DEPTH) ** 0.25
EPS, RMS_EPS = 1e-5, 1e-6
A_SCALE, HEAD_SCALE = (HD // 2) ** -0.5, HD ** -0.5
LAM_INIT = [0.8 - 0.6 * math.exp(-0.3 * layer) for layer in range(DEPTH)]
MASKED = -1.0e30
GRID_W, NA_KW, RPB_H, RPB_W = 64, 16, 15, 31
D_FF = 5632
FF = D_FF // COLS
N_MOD = 6
MOD_GROUPS = N_MOD * D // COLS
POOL_WINDOWS = (2, 4, 8, 16)

RING = 4
TILES_PER_BAR = 8
GROUPS_1 = 15
L1_BARS, L2_BARS, LAST_BARS, L3_BARS, OUT_BARS = 12, 32, 2, 8, 8
LAYER_BARS = L1_BARS + L2_BARS + LAST_BARS + L3_BARS + OUT_BARS
AT_L2 = L1_BARS
AT_LAST = AT_L2 + L2_BARS
AT_L3 = AT_LAST + LAST_BARS
AT_OUT = AT_L3 + L3_BARS
AT_KVC = DEPTH * LAYER_BARS
AT_IN2 = AT_KVC + 8
AT_GATES = AT_IN2 + 22
AT_GATE0 = AT_GATES + 30
AT_NAP = AT_GATE0 + 8
AT_WO = AT_NAP + 4
AT_FF = AT_WO + 8
BARS = AT_FF + 6 * FF

BQ, BK, BV, AQ, AK, AV, CU, CGLU, GATE = 0, 1024, 2048, 3072, 3584, 4096, 4608, 5120, 5632
W1 = GROUPS_1 * COLS
NQ, NK, NV, FT, POOL, SV, SB, SC = 0, 1024, 2048, 3072, 3584, 4096, 4608, 5120
W2 = 11 * COLS
Y2 = POOL


DVE_B, DVE_A, DVE_GATES, DVE_LAYER = 3, 6, (6, 8, 2), 57

VECS = (("c_cols", 2 * KT), ("b_mod", 2 * N_MOD * KT), ("rel_bias", A_HEADS + B_HEADS), ("head_gain", DEPTH * HD),
        ("conv_dw", DEPTH * 4 * CONV), ("conv_b", DEPTH * 4), ("conv_g", DEPTH * 4), ("conv_beta", DEPTH * 4),
        ("norm1", 2 * KT), ("norm2", KT), ("q_norm", 1), ("k_norm", 1), ("pool_scale", 4), ("short_w", 12))


class Chain:

    def __init__(self, eng, sem):
        self.eng, self.sem, self.base, self.n = eng, sem, 0, 0

    def link(self, ins):
        ins.then_inc(self.sem, 1)
        self.n += 1
        self.eng.wait_ge(self.sem, self.base + self.n)

    @contextmanager
    def loop(self, i, rounds, steps):
        base, n = self.base, self.n
        self.base, self.n = i * steps + n + base, 0
        yield
        assert self.n == steps, (self.n, steps)
        self.base, self.n = base, n + rounds * steps


def build(nc, stream, x_in, consts, vecs, lam_rows, rpb, ctx_in, ln_gb, conv_pw, cs_dft, inv_cnt, w_pool, scratch, out):
    with ExitStack() as ctx:
        def sb(name, shape, dt=F32):
            return ctx.enter_context(nc.sbuf_tensor(name, shape, dt))

        def sem(name):
            return ctx.enter_context(nc.semaphore(name))

        raw = sb("raw", [P, RING, 2 * COLS])
        w_hi = sb("w_hi", [P, RING, 2 * COLS], F32R)
        w_lo = sb("w_lo", [P, RING, 2 * COLS], F32R)
        act_hi = sb("act_hi", [P, KT, S], F32R)
        act_lo = sb("act_lo", [P, KT, S], F32R)
        br_hi = sb("br_hi", [P, 4, S], F32R)
        br_lo = sb("br_lo", [P, 4, S], F32R)
        cs = sb("cs", [P, KT, 4], F32R)
        x = sb("x", [P, TT, D])
        flat = sb("flat", [P, TT * W1])
        p1 = flat[:, :].rearrange("p (t c) -> p t c", t=TT)
        p2 = flat[:, 0:TT * W2].rearrange("p (t c) -> p t c", t=TT)
        kvc = flat[:, TT * W2:TT * W1].rearrange("p (t c) -> p t c", t=TT)
        ctx_tok = flat[:, 0:TT * D].rearrange("p (t c) -> p t c", t=TT)
        xn = flat[:, TT * D:2 * TT * D].rearrange("p (t c) -> p t c", t=TT)
        rpb_rows = flat[:, 2 * TT * D:2 * TT * D + 2048]
        shared = sb("shared", [P, 4096])
        bias_t = shared[:, 0:3072]
        conv_acc = shared[:, 3072:4096].rearrange("p (j t) -> p j t", j=4)
        na_bias = shared[:, :].rearrange("p (q n) -> p q n", q=TT)
        dft = shared[:, 0:1280]
        head = sb("head", [P, 2688])
        stage = head[:, 0:768].rearrange("p (i d) -> p i d", d=HD)
        qkt = head[:, 768:1536]
        probs = head[:, 1536:2560]
        p_t = head[:, 2304:2688]
        na_pt = head[:, 0:1024]
        pool_u = head[:, 0:1088].rearrange("p (g t) -> p g t", g=4)
        pool_p = head[:, 1088:2112].rearrange("p (g t) -> p g t", g=4)
        pool_s = [head[:, 2112 + 272 * i:2112 + 272 * (i + 1)] for i in range(2)]
        gtmp = sb("gtmp", [P, TT, COLS])
        gflat = gtmp[:, :, :].rearrange("p t c -> p (t c)")
        mod_row = gtmp[0:4, 0, :]
        junk = gtmp[:, 1, :].rearrange("p (t d) -> p t d", d=HD)
        lam_in = gtmp[:, 1, :]
        conv_pad = sb("conv_pad", [P, 4, 288])
        pool_v = conv_pad[:, :, :].rearrange("p j t -> p (j t)")[:, 0:1024].rearrange("p (j t) -> p j t", j=4)
        C = sb("consts_sb", [P, consts.shape[1]])
        V = sb("vecs_sb", [P, vecs.shape[1]])
        mod_t = sb("mod_t", [P, 2 * N_MOD * KT])
        mod3 = mod_t[:, :].rearrange("p (n c) -> p n c", c=2)
        hs1 = sb("hs1", [P, KT, 2])
        hs2 = sb("hs2", [P, KT])
        csf = sb("csf", [P, KT * 2])
        lam = sb("lam", [P, 8])
        small = sb("small", [P, 64])
        stats = sb("stats", [P, 4, 4 * 6])
        mv = sb("mv", [P, 4, 2])
        ms = sb("ms", [P, 48])
        rstd = sb("rstd", [P, 48])
        half = sb("half", [P, 48])
        ss = sb("ss", [P, 48])
        ones = sb("ones", [P, P])
        nm, sums, recip, nlr, mx = (small[:, 8 * i:8 * i + 4] for i in range(5))

        ident, flip = C[:, 0:128], C[:, 128:256]
        na_mask = C[:, 256:320]
        comb = C[0:4, 320:322]
        onehot, mask_r = gtmp[0:N_BUCKETS, 0, 0:384], head[0:12, 0:384]
        rvec = head[0:12, 384:768]
        o = 0
        vec = {}
        for name, n in VECS:
            vec[name] = V[:, o:o + n]
            o += n

        ps = [ctx.enter_context(nc.psum_tensor(f"ps{i}", [P, COLS], F32)) for i in range(8)]

        landed = [sem(f"landed{i}") for i in range(RING)]
        hi_ready, lo_ready = sem("hi_ready"), sem("lo_ready")
        chunk_used = sem("chunk_used")
        x_landed, consts_landed = sem("x_landed"), sem("consts_landed")
        rel_ready, rvec_ready, rvec_stored, rows_landed = sem("rel_ready"), sem("rvec_ready"), sem("rvec_stored"), sem("rows_landed")
        rows_flipped, bias_ready = sem("rows_flipped"), sem("bias_ready")
        csf_ready, cs_ready, lam_dots, lam_exp = sem("csf_ready"), sem("cs_ready"), sem("lam_dots"), sem("lam_exp")
        cleared = sem("cleared")
        turned, turn_hi, turn_lo = sem("turned"), sem("turn_hi"), sem("turn_lo")
        evac_a, evac_d = sem("evac_a"), sem("evac_d")
        qk_staged, qkt_ready, qkt_copied = sem("qk_staged"), sem("qkt_ready"), sem("qkt_copied")
        scores_ready, max_ready, exps_ready = sem("scores_ready"), sem("max_ready"), sem("exps_ready")
        diff_ready, pt_ready, pt_copied = sem("diff_ready"), sem("pt_ready"), sem("pt_copied")
        pv_ready, squares_ready, head_done = sem("pv_ready"), sem("squares_ready"), sem("head_done")
        mod_row_ready, mod_col_ready, mod_done = sem("mod_row_ready"), sem("mod_col_ready"), sem("mod_done")
        ms_ready, rstd_ready = sem("ms_ready"), sem("rstd_ready")
        conv_tapped = sem("conv_tapped")
        glu_sig, glu_ready, cu_turned, conv_in = sem("glu_sig"), sem("glu_ready"), sem("cu_turned"), sem("conv_in")
        gates_ready, conv_turned, cn_ready = sem("gates_ready"), sem("conv_turned"), sem("cn_ready")
        cn_turned, conv_act, cpw_landed, cpw_ready = sem("cn_turned"), sem("conv_act"), sem("cpw_landed"), sem("cpw_ready")
        y_ready, ln_landed, x_ready = sem("y_ready"), sem("ln_landed"), sem("x_ready")
        x_summed = sem("x_summed")
        ctx_landed, rpb_landed, na_flipped, na_biased = sem("ctx_landed"), sem("rpb_landed"), sem("na_flipped"), sem("na_biased")
        scale_ready, ctx_ready, xn_ready = sem("scale_ready"), sem("ctx_ready"), sem("xn_ready")
        u_ready, u_turned, u_copied, pool_turned, pool_copied = sem("u_ready"), sem("u_turned"), sem("u_copied"), sem("pool_turned"), sem("pool_copied")
        inv_landed, wp_landed, pool_ready, pool_out, pool_scaled = sem("inv_landed"), sem("wp_landed"), sem("pool_ready"), sem("pool_out"), sem("pool_scaled")
        br_ready = sem("br_ready")
        sig_done, gate_added = sem("sig_done"), sem("gate_added")
        dft_landed, ft_cols, ft_copied, ft_ready = sem("dft_landed"), sem("ft_cols"), sem("ft_copied"), sem("ft_ready")
        diag_ready, row_ready, row_copied = sem("diag_ready"), sem("row_ready"), sem("row_copied")
        h2_ready = sem("h2_ready")
        silu_done, hid_ready, hid_turned, hid_hi, hid_lo = sem("silu_done"), sem("hid_ready"), sem("hid_turned"), sem("hid_hi"), sem("hid_lo")
        acc_done = sem("acc_done")
        out_ready, stored = sem("out_ready"), sem("stored")
        dve_chain = sem("dve_chain")

        TURN_X0, TURN_KVC = 0, 8 + 16 * DEPTH
        TURN_H, TURN_NA = TURN_KVC + 8, TURN_KVC + 16
        TURN_Y2, TURN_H2 = TURN_NA + 4, TURN_NA + 12

        block = ctx.enter_context(nc.Block())

        @block.sync
        def _(sp):
            sp.dma_start(x[:, :, :], x_in.rearrange("(t p) d -> p t d", p=P)).then_inc(x_landed, 16)
            for j in range(RING):
                sp.dma_start(raw[:, j, :], stream[0, :, j * 1024:(j + 1) * 1024]).then_inc(landed[j], 16)
            with sp.Fori(1, BARS) as bar:
                for j in range(RING):
                    sp.wait_ge(lo_ready, 4 * bar + j - 3)
                    sp.wait_ge(x_landed, 16)
                    sp.dma_start(raw[:, j, :], stream[bass.ds(bar, 1), :, j * 1024:(j + 1) * 1024])\
                        .then_inc(landed[j], 16)
            for t in range(TT):
                sp.wait_ge(out_ready, t + 1)
                sp.dma_start(out[t * P:(t + 1) * P, :], x[:, t, :]).then_inc(stored, 16)
            sp.wait_ge(stored, 16 * TT)

        @block.gpsimd
        def _(pool):
            pool.memset(half[:, :], -0.5).then_inc(cleared, 1)
            pool.memset(conv_pad[:, :, :], 0.0).then_inc(cleared, 1)
            pool.memset(ones[:, :], 1.0).then_inc(cleared, 1)
            for k, (count, start) in enumerate(((evac_a, 2), (evac_d, 2), (x_summed, 2), (acc_done, 2), (sig_done, 1), (gate_added, 1))):
                pool.memset(small[:, 48 + k:49 + k], 0.0).then_inc(count, start)
            pool.wait_ge(cleared, 3)

            def inverse_root(index, cols):
                pool.wait_ge(ms_ready, index + 1)
                pool.tensor_tensor(rstd[:, 0:cols], ms[:, 0:cols], half[:, 0:cols], ALU.pow).then_inc(rstd_ready, 1)

            with pool.Fori(0, DEPTH) as L:
                pool.wait_ge(head_done, L * 12 + B_HEADS)
                pool.wait_ge(cleared, 3)
                for t in range(2):
                    row = bass.AP(ln_gb.tensor, L * (2 * D) + t * D, [[0, P], [1, D]])
                    pool.dma_start(p1[:, t, BK:BK + D], row).then_inc(ln_landed, 16)
                pool.wait_ge(cu_turned, L + 1)
                pool.wait_ge(cleared, 3)
                for j in range(4):
                    at = CU + (j % 2) * COLS
                    pool.dma_start(p1[:, j // 2, at:at + COLS],
                                   conv_pw[bass.ds(L * 4 + j, 1), :, :]).then_inc(cpw_landed, 16)
                with pool.Fori(0, A_HEADS) as h:
                    inverse_root(L * 6 + h, 2)
                inverse_root(L * 6 + 4, 2)
                inverse_root(L * 6 + 5, 2)

            pool.wait_ge(turn_lo, TURN_KVC)
            pool.dma_start(ctx_tok, ctx_in.rearrange("(t p) d -> p t d", p=P)).then_inc(ctx_landed, 16)
            for q in range(TT):
                if q:
                    pool.wait_ge(na_flipped, 4)
                for r in range(2):
                    half_rows = rpb_rows[P - 64 * (r + 1):P - 64 * r, :]
                    with pool.Fori(0, NA_HEADS) as h:
                        src = bass.AP(rpb.tensor, h * (RPB_H * RPB_W) + (7 - 2 * q - r) * RPB_W - 48,
                                      [[1, 64], [RPB_W, 4], [1, GRID_W]])
                        dst = half_rows[:, bass.ds(h * 256, 256)].rearrange("p (a c) -> p a c", a=4)
                        pool.dma_start(dst, src).then_inc(rpb_landed, 16)
            pool.dma_start(pool_p, inv_cnt).then_inc(inv_landed, 16)
            inverse_root(12, 4)
            inverse_root(13, 48)
            pool.wait_ge(u_turned, 1)
            pool.dma_start(p2[:, 0, SV:SV + COLS], w_pool).then_inc(wp_landed, 16)
            pool.wait_ge(head_done, 24 + NA_HEADS)
            pool.dma_start(dft, cs_dft).then_inc(dft_landed, 16)
            inverse_root(14, 2)

        @block.scalar
        def _(act):

            def split(bar, s):
                act.wait_ge(landed[s % RING], 16 * (bar + s // RING + 2))
                act.wait_ge(chunk_used, 4 * bar + s + 1)
                nc.scalar.activation(w_hi[:, s % RING, :], raw[:, s % RING, :], ACT.Copy).then_inc(hi_ready, 1)

            def turn(first, rounds=8):
                for r in range(rounds):
                    act.wait_ge(turned, first + r + 1)
                    nc.scalar.activation(act_hi[:, 2 * r:2 * r + 2, :], ps[4 + r % 4][:, :].rearrange("p (k t) -> p k t", k=2),
                                         ACT.Copy).then_inc(turn_hi, 1)

            def turn_modulated(first, scale, shift):
                for r in range(8):
                    act.wait_ge(turned, first + r + 1)
                    if r >= 2:
                        act.wait_ge(turn_lo, first + r - 1)
                    for k in range(2):
                        kt = 2 * r + k
                        ins = nc.scalar.activation(gtmp[:, r % 2, k * S:(k + 1) * S], ps[4 + r % 4][:, k * S:(k + 1) * S],
                                                   ACT.Identity, scale=scale(kt), bias=shift(kt))
                    ins.then_inc(turn_hi, 1)

            act.dma_start(C[:, :], consts[0:P, :]).then_inc(consts_landed, 16)
            act.dma_start(V[:, :], vecs).then_inc(consts_landed, 16)
            act.dma_start(onehot, consts[P:P + N_BUCKETS, 0:384]).then_inc(consts_landed, 16)
            act.dma_start(mask_r, consts[P + N_BUCKETS:P + N_BUCKETS + 12, 0:384]).then_inc(consts_landed, 16)
            act.dma_start(lam_in, bass.AP(lam_rows.tensor, 0, [[0, P], [1, DEPTH * 256]])).then_inc(consts_landed, 16)
            for j in range(RING):
                act.wait_ge(landed[j], 16)
                nc.scalar.activation(w_hi[:, j, :], raw[:, j, :], ACT.Copy).then_inc(hi_ready, 1)
            act.wait_ge(consts_landed, 80)
            nc.scalar.activation(csf[:, :], vec["c_cols"], ACT.Silu).then_inc(csf_ready, 1)
            act.wait_ge(lam_dots, 1)
            nc.scalar.activation(lam[:, 4:8], lam[:, 0:4], ACT.Exp).then_inc(lam_exp, 1)
            act.wait_ge(rvec_ready, 1)
            act.dma_start(scratch, rvec).then_inc(rvec_stored, 16)
            act.wait_ge(rvec_stored, 16)
            act.dma_start(flat[:, 0:3072].rearrange("p (h c) -> p h c", h=12),
                          bass.AP(scratch.tensor, 0, [[1, P], [384, 12], [1, S]])).then_inc(rows_landed, 16)
            turn(TURN_X0)
            for r in range(6):
                act.wait_ge(rows_flipped, r + 1)
                ins = nc.scalar.activation(bias_t[:, r * 512:(r + 1) * 512], ps[r % 4][:, :], ACT.Copy)
                ins.then_inc(bias_ready, 1)

            def copy_group(bank, dst, count=evac_a):
                nc.scalar.activation(dst, ps[bank][:, :], ACT.Copy).then_inc(count, 1)

            def stage_heads(H, q_at, k_at):
                nc.scalar.activation(stage[:, 0:2, :], p1[:, :, bass.ds(q_at, HD)], ACT.Copy)
                nc.scalar.activation(stage[:, 2:4, :], p1[:, :, bass.ds(k_at, HD)], ACT.Copy).then_inc(qk_staged, 1)

            def copy_qkt(H):
                act.wait_ge(qkt_ready, H + 1)
                nc.scalar.activation(qkt[:, 0:512], ps[4][:, :], ACT.Copy).then_inc(qkt_copied, 1)

            def exps(H, parts):
                act.wait_ge(max_ready, H + 1)
                for i, (a, b) in enumerate(parts):
                    ins = nc.scalar.activation(probs[:, a:b], probs[:, a:b], ACT.Exp, bias=nm[:, i:i + 1],
                                               accum_out=sums[:, i:i + 1])
                ins.then_inc(exps_ready, 1)

            def copy_pt(H):
                act.wait_ge(pt_ready, H + 1)
                nc.scalar.activation(p_t, ps[6][:, 0:384], ACT.Copy).then_inc(pt_copied, 1)

            def copy_mod_row():
                nc.scalar.activation(mod_row, ps[2][0:4, :], ACT.Copy).then_inc(mod_row_ready, 1)

            with act.Fori(0, DEPTH) as L:
                B0 = L * LAYER_BARS
                with act.Fori(0, 3) as i:
                    for p in range(2):
                        for s in range(8):
                            split(B0 + 4 * i + 2 * p, s)
                        copy_group(2 * p, p1[:, 0, bass.ds((2 * i + p) * COLS, COLS)])
                with act.Fori(0, B_HEADS) as h:
                    H = L * 12 + h
                    for s in range(16):
                        split(B0 + AT_L2 + 4 * h, s)
                        if s == 0:
                            act.wait_ge(evac_a, L * GROUPS_1 + 8)
                            act.wait_ge(evac_d, L * GROUPS_1 + 8)
                            stage_heads(H, BQ + h * HD, BK + h * HD)
                        if s == 1:
                            copy_qkt(H)
                        if s == 4:
                            exps(H, [(0, 128), (128, 384)])
                        if s == 8:
                            copy_pt(H)
                    copy_mod_row()
                    copy_group(0, p1[:, 0, bass.ds(AQ + h * COLS, COLS)])
                for s in range(8):
                    split(B0 + AT_LAST, s)
                    if s == 0:
                        act.wait_ge(evac_a, L * GROUPS_1 + 16)
                        act.wait_ge(evac_d, L * GROUPS_1 + 16)
                        nc.scalar.activation(p1[:, :, CGLU:CGLU + D_C], p1[:, :, CGLU:CGLU + D_C], ACT.Sigmoid)\
                            .then_inc(glu_sig, 1)
                    if s == 1:
                        act.wait_ge(cu_turned, L + 1)
                        for k in range(2):
                            ins = nc.scalar.activation(conv_pad[:, 2 * k:2 * k + 2, CONV - 1:CONV - 1 + S],
                                                       ps[4 + k][:, :].rearrange("p (j t) -> p j t", j=2), ACT.Copy)
                        ins.then_inc(conv_in, 1)
                copy_group(0, p1[:, 0, GATE + 3 * COLS:GATE + 4 * COLS])
                act.wait_ge(evac_a, L * GROUPS_1 + 17)
                act.wait_ge(evac_d, L * GROUPS_1 + 17)
                nc.scalar.activation(p1[:, 0, GATE:W1], p1[:, 0, GATE:W1], ACT.Silu)
                nc.scalar.activation(p1[:, 1, GATE:W1], p1[:, 1, GATE:W1], ACT.Silu).then_inc(gates_ready, 1)
                with act.Fori(0, A_HEADS) as h:
                    H = L * 12 + B_HEADS + h
                    for s in range(8):
                        split(B0 + AT_L3 + 2 * h, s)
                        if s == 0:
                            stage_heads(H, AQ + h * HD, AK + h * HD)
                        if s == 1:
                            copy_qkt(H)
                        if s == 3:
                            exps(H, [(0, 128), (128, 384), (384, 512), (512, 768)])
                        if s == 5:
                            copy_pt(H)
                        if s == 6:
                            act.wait_ge(pv_ready, H + 1)
                            for t in range(TT):
                                ins = nc.scalar.activation(junk[:, t, :], ps[7][:, t * HD:(t + 1) * HD], ACT.Square,
                                                           accum_out=ss[:, t:t + 1])
                            ins.then_inc(squares_ready, 1)
                    copy_mod_row()
                act.wait_ge(cn_turned, L + 1)
                for j in range(4):
                    ins = nc.scalar.activation(conv_acc[:, j, :], ps[6 + j // 2][:, (j % 2) * S:(j % 2 + 1) * S], ACT.Silu,
                                               scale=vec["conv_g"][:, bass.ds(L * 4 + j, 1)],
                                               bias=vec["conv_beta"][:, bass.ds(L * 4 + j, 1)])
                ins.then_inc(conv_act, 1)
                turn(8 + 16 * L)
                with act.Fori(0, 2) as i:
                    for p in range(2):
                        for s in range(8):
                            split(B0 + AT_OUT + 4 * i + 2 * p, s)
                turn(16 + 16 * L)

            act.wait_ge(scale_ready, 1)
            turn_modulated(TURN_KVC, lambda k: hs1[:, k, 1:2], lambda k: mod3[:, k, 1:2])
            with act.Fori(0, 2) as i:
                for p in range(2):
                    for s in range(8):
                        split(AT_KVC + 4 * i + 2 * p, s)
                    copy_group(2 * p, kvc[:, 0, bass.ds((2 * i + p) * COLS, COLS)])
            turn_modulated(TURN_H, lambda k: hs1[:, k, 0:1], lambda k: mod3[:, k, 0:1])
            with act.Fori(0, 5) as i:
                for p in range(2):
                    for s in range(8):
                        split(AT_IN2 + 4 * i + 2 * p, s)
                    copy_group(2 * p, p2[:, 0, bass.ds((2 * i + p) * COLS, COLS)])
            for s in range(8):
                split(AT_IN2 + 20, s)
            copy_group(0, p2[:, 0, SC:SC + COLS])
            act.wait_ge(u_turned, 1)
            for k in range(2):
                ins = nc.scalar.activation(conv_pad[:, 2 * k:2 * k + 2, CONV - 1:CONV - 1 + S],
                                           ps[4 + k][:, :].rearrange("p (j t) -> p j t", j=2), ACT.Copy)
            ins.then_inc(u_copied, 1)
            act.wait_ge(pool_turned, 1)
            act.wait_ge(cleared, 4)
            for k in range(2):
                ins = nc.scalar.activation(pool_u[:, 2 * k:2 * k + 2, 8:8 + S],
                                           ps[k][:, :].rearrange("p (j t) -> p j t", j=2), ACT.Copy)
            ins.then_inc(pool_copied, 1)
            act.wait_ge(pool_out, 1)
            act.wait_ge(br_ready, 1)
            for g in range(4):
                ins = nc.scalar.activation(pool_v[:, g, :], ps[4 + g // 2][:, (g % 2) * S:(g % 2 + 1) * S], ACT.Copy,
                                           scale=vec["pool_scale"][:, g:g + 1])
            ins.then_inc(pool_scaled, 1)

            def na_stage(h):
                for i, src in enumerate([p2[:, 0], p2[:, 1]]):
                    nc.scalar.activation(stage[:, i, :], src[:, bass.ds(NQ + h * HD, HD)], ACT.Copy,
                                         scale=rstd[:, bass.ds(8 * i + h, 1)])
                    nc.scalar.activation(stage[:, 2 + i, :], src[:, bass.ds(NK + h * HD, HD)], ACT.Copy,
                                         scale=rstd[:, bass.ds(8 * (2 + i) + h, 1)])
                    ins = nc.scalar.activation(stage[:, 4 + i, :], kvc[:, i, bass.ds(h * HD, HD)], ACT.Copy,
                                               scale=rstd[:, bass.ds(8 * (4 + i) + h, 1)])
                ins.then_inc(qk_staged, 1)

            for turn_of, branch in enumerate((3, 2, 1)):
                with act.Fori(0, 2) as i:
                    for s in range(20):
                        n, r = 2 * i + s // 10, s % 10
                        g = 4 * turn_of + n
                        H = 24 + g
                        split(AT_GATES + 10 * turn_of + 5 * i, s)
                        if r == 7:
                            act.wait_ge(gate_added, g + 1)
                            nc.scalar.activation(gtmp[:, 0, :], ps[0][:, :], ACT.Sigmoid)
                            nc.scalar.activation(gtmp[:, 1, :], ps[1][:, :], ACT.Sigmoid).then_inc(sig_done, 1)
                        if turn_of == 2:
                            continue
                        if r == 0:
                            act.wait_ge(pv_ready, H)
                            act.wait_ge(rstd_ready, 14)
                            na_stage(g)
                        if r == 1:
                            act.wait_ge(qkt_ready, H + 1)
                            nc.scalar.activation(qkt[:, 0:256], ps[4][:, 0:256], ACT.Copy, scale=vec["q_norm"][:, 0:1])
                            nc.scalar.activation(qkt[:, 256:512], ps[4][:, 256:512], ACT.Copy, scale=vec["k_norm"][:, 0:1])
                            nc.scalar.activation(qkt[:, 512:768], ps[5][:, 0:256], ACT.Copy, scale=vec["k_norm"][:, 0:1])\
                                .then_inc(qkt_copied, 1)
                        if r == 3:
                            exps(H, [(0, 512), (512, 1024)])
                        if r == 6:
                            act.wait_ge(pt_ready, H + 1)
                            nc.scalar.activation(na_pt[:, 0:512], ps[4][:, :], ACT.Copy)
                            nc.scalar.activation(na_pt[:, 512:1024], ps[5][:, :], ACT.Copy).then_inc(pt_copied, 1)
                if turn_of == 1:
                    for g in range(4):
                        act.wait_ge(ft_cols, g + 1)
                        nc.scalar.activation(p2[:, g // 2, NK + (g % 2) * COLS:NK + (g % 2 + 1) * COLS], ps[4 + g][:, :],
                                             ACT.Copy).then_inc(ft_copied, 1)
                    for r in range(8):
                        act.wait_ge(row_ready, r + 1)
                        if r == 4:
                            act.wait_ge(ft_ready, 1)
                        at = (NV, NK)[r // 4] + (r % 2) * COLS
                        nc.scalar.activation(p2[:, (r % 4) // 2, at:at + COLS], ps[6 + r % 2][:, :], ACT.Copy)\
                            .then_inc(row_copied, 1)
            with act.Fori(0, 2) as i:
                for p in range(2):
                    for s in range(8):
                        split(AT_GATE0 + 4 * i + 2 * p, s)
                    for t in range(TT):
                        ins = nc.scalar.activation(kvc[:, t, bass.ds((2 * i + p) * COLS, COLS)], ps[2 * p + t][:, :], ACT.Sigmoid)
                    ins.then_inc(sig_done, 1)
            turn(TURN_NA, 4)
            with act.Fori(0, 2) as i:
                for s in range(8):
                    split(AT_NAP + 2 * i, s)
            turn(TURN_Y2)
            with act.Fori(0, 2) as i:
                for p in range(2):
                    for s in range(8):
                        split(AT_WO + 4 * i + 2 * p, s)
            act.wait_ge(scale_ready, 2)
            turn_modulated(TURN_H2, lambda k: hs2[:, k:k + 1], lambda k: mod3[:, 3 * KT + k, 0:1])

            def silus():
                for t in range(TT):
                    ins = nc.scalar.activation(gtmp[:, t, :], ps[t][:, :], ACT.Silu)
                ins.then_inc(silu_done, 1)

            def hidden_hi(f):
                act.wait_ge(hid_turned, f + 1)
                for k in range(2):
                    ins = nc.scalar.activation(br_hi[:, 2 * k:2 * k + 2, :], ps[4 + k][:, :].rearrange("p (j t) -> p j t", j=2), ACT.Copy)
                ins.then_inc(hid_hi, 1)

            for s in range(16):
                split(AT_FF, s)
                if s == 7:
                    act.wait_ge(turn_lo, TURN_H2 + 8)
                    silus()
            with act.Fori(0, FF - 1) as i:
                for s in range(24):
                    split(AT_FF + 4 + 6 * i, s)
                    if s == 7:
                        act.wait_ge(hid_ready, i + 1)
                        silus()
                        hidden_hi(i)
            hidden_hi(FF - 1)
            for s in range(4):
                split(BARS - 2, s)

        @block.tensor
        def _(pe):
            def chunk(bar, s, tiles):
                pe.wait_ge(lo_ready, 4 * bar + s + 1)
                for u, (hi, lo, kt, banks, first, last) in enumerate(tiles):
                    wh = w_hi[:, s % RING, u * COLS:(u + 1) * COLS]
                    wl = w_lo[:, s % RING, u * COLS:(u + 1) * COLS]
                    for t in range(TT):
                        xh, xl = hi[:, kt, t * P:(t + 1) * P], lo[:, kt, t * P:(t + 1) * P]
                        acc = ps[banks[t]][:, :]
                        nc.tensor.matmul(acc, xh, wh, start=first, stop=False)
                        nc.tensor.matmul(acc, xh, wl, start=False, stop=False)
                        mm = nc.tensor.matmul(acc, xl, wh, start=False, stop=last)
                mm.then_inc(chunk_used, 1)

            def of_group(s, banks, tiles=KT, hi=None, lo=None):
                hi, lo = (act_hi, act_lo) if hi is None else (hi, lo)
                return [(hi, lo, 2 * s + u, banks, 2 * s + u == 0, 2 * s + u == tiles - 1) for u in range(2)]

            def mod_chunk(bar, s, k):
                pe.wait_ge(lo_ready, 4 * bar + s + 1)
                for u in range(2):
                    kt = 2 * k + u
                    for w in (w_hi, w_lo):
                        mm = nc.tensor.matmul(ps[2][0:4, :], cs[:, kt, :], w[:, s % RING, u * COLS:(u + 1) * COLS],
                                              start=kt == 0 and w is w_hi, stop=kt == KT - 1 and w is w_lo)
                mm.then_inc(chunk_used, 1)

            def mod_columns(M):
                pe.wait_ge(mod_row_ready, M + 1)
                for j in range(4):
                    mm = nc.tensor.matmul(ps[3][:, 2 * j:2 * j + 2], mod_row[:, j * P:(j + 1) * P], comb, start=True, stop=True)
                mm.then_inc(mod_col_ready, 1)

            def turn(first, src, rounds=8):
                for r in range(rounds):
                    if r >= 4:
                        pe.wait_ge(turn_lo, first + r - 3)
                    for k in range(2):
                        for t in range(TT):
                            at = k * S + t * P
                            mm = nc.tensor.transpose(ps[4 + r % 4][:, at:at + P], src(t, 2 * r + k), ident)
                    mm.then_inc(turned, 1)

            def turn_cols(banks, src, count=None):
                for j in range(4):
                    for t in range(TT):
                        at = (j % 2) * S + t * P
                        mm = nc.tensor.transpose(ps[banks[j // 2]][:, at:at + P], src(t, j), ident)
                if count is not None:
                    mm.then_inc(count, 1)

            pe.wait_ge(consts_landed, 80)
            nc.tensor.matmul(ps[0][0:12, 0:384], vec["rel_bias"][0:N_BUCKETS, :], onehot, start=True, stop=True).then_inc(rel_ready, 1)
            pe.wait_ge(x_landed, 16)
            turn(TURN_X0, lambda t, k: x[:, t, k * P:(k + 1) * P])
            pe.wait_ge(rows_landed, 16)
            for r in range(6):
                if r >= 4:
                    pe.wait_ge(bias_ready, r - 3)
                nc.tensor.matmul(ps[r % 4][:, :], flip, flat[:, r * 512:(r + 1) * 512], start=True, stop=True).then_inc(rows_flipped, 1)
            pe.wait_ge(bias_ready, 6)
            pe.wait_ge(cs_ready, 1)
            pe.wait_ge(turn_lo, 8)

            def turn_heads(H, n=4):
                pe.wait_ge(qk_staged, H + 1)
                for i in range(n):
                    mm = nc.tensor.transpose(ps[4 + i // 4][:, (i % 4) * P:(i % 4 + 1) * P], stage[:, i, :], ident)
                mm.then_inc(qkt_ready, 1)

            def scores(bank, rows):
                q, k = qkt[rows, 0:256], qkt[rows, 256:512]
                nc.tensor.matmul(ps[bank][:, 0:128], q[:, 0:128], k[:, 0:128], start=True, stop=True)
                return nc.tensor.matmul(ps[bank][:, 128:384], q[:, 128:256], k, start=True, stop=True)

            def turn_probs():
                for i in range(3):
                    mm = nc.tensor.transpose(ps[6][:, i * P:(i + 1) * P], probs[:, i * P:(i + 1) * P], ident)
                mm.then_inc(pt_ready, 1)

            def weigh_values(H, at):
                pe.wait_ge(pt_copied, H + 1)
                v = [p1[:, t, bass.ds(at, HD)] for t in range(TT)]
                nc.tensor.matmul(ps[7][:, 0:HD], p_t[:, 0:128], v[0], start=True, stop=True)
                nc.tensor.matmul(ps[7][:, HD:2 * HD], p_t[:, 128:256], v[0], start=True, stop=False)
                nc.tensor.matmul(ps[7][:, HD:2 * HD], p_t[:, 256:384], v[1], start=False, stop=True).then_inc(pv_ready, 1)

            with pe.Fori(0, DEPTH) as L:
                B0 = L * LAYER_BARS
                with pe.Fori(0, 3) as i:
                    for p in range(2):
                        for e in (evac_a, evac_d):
                            pe.wait_ge(e, L * GROUPS_1 + 2 * i + p + 1)
                        for s in range(8):
                            chunk(B0 + 4 * i + 2 * p, s, of_group(s, (2 * p, 2 * p + 1)))
                with pe.Fori(0, B_HEADS) as h:
                    H, bar = L * 12 + h, B0 + AT_L2 + 4 * h
                    for e in (evac_a, evac_d):
                        pe.wait_ge(e, L * GROUPS_1 + 6 + 2)
                    for s in range(16):
                        if s == 1:
                            for e in (evac_a, evac_d):
                                pe.wait_ge(e, L * GROUPS_1 + 6 + 2 + h)
                        if s % 2:
                            chunk(bar, s, of_group(s // 2, (0, 1)))
                        else:
                            mod_chunk(bar, s, s // 2)
                        if s == 1:
                            turn_heads(H)
                        if s == 4:
                            pe.wait_ge(qkt_copied, H + 1)
                            scores(5, slice(0, P)).then_inc(scores_ready, 1)
                        if s == 8:
                            pe.wait_ge(exps_ready, H + 1)
                            turn_probs()
                        if s == 11:
                            weigh_values(H, BV + h * HD)
                    mod_columns(L * 12 + h)
                for e in (evac_a, evac_d):
                    pe.wait_ge(e, L * GROUPS_1 + 14 + 2)
                for s in range(8):
                    chunk(B0 + AT_LAST, s, of_group(s, (0, 1)))
                    if s == 1:
                        pe.wait_ge(glu_ready, L + 1)
                        turn_cols((4, 5), lambda t, j: p1[:, t, CU + j * P:CU + (j + 1) * P], cu_turned)
                with pe.Fori(0, A_HEADS) as h:
                    H = L * 12 + B_HEADS + h
                    for s in range(8):
                        mod_chunk(B0 + AT_L3 + 2 * h, s, s)
                        if s == 0:
                            turn_heads(H)
                        if s == 2:
                            pe.wait_ge(qkt_copied, H + 1)
                            scores(5, slice(0, 64))
                            scores(6, slice(64, 128)).then_inc(scores_ready, 1)
                        if s == 5:
                            pe.wait_ge(diff_ready, L * A_HEADS + h + 1)
                            turn_probs()
                        if s == 6:
                            weigh_values(H, AV + h * HD)
                    mod_columns(L * 12 + B_HEADS + h)
                pe.wait_ge(conv_tapped, CONV * (L + 1))
                for t in range(TT):
                    for j in range(4):
                        mm = nc.tensor.transpose(ps[4 + t][:, j * P:(j + 1) * P], conv_acc[:, j, t * P:(t + 1) * P], ident)
                mm.then_inc(conv_turned, 1)
                pe.wait_ge(cn_ready, L + 1)
                turn_cols((6, 7), lambda t, j: p1[:, t, AK + j * P:AK + (j + 1) * P], cn_turned)
                pe.wait_ge(conv_act, L + 1)
                pe.wait_ge(cpw_landed, 64 * (L + 1))
                pe.wait_ge(conv_act, 1)
                for t in range(TT):
                    for j in range(4):
                        at = CU + (j % 2) * COLS
                        mm = nc.tensor.matmul(ps[t][:, :], conv_acc[:, j, t * P:(t + 1) * P], p1[:, j // 2, at:at + COLS],
                                              start=j == 0, stop=j == 3)
                mm.then_inc(cpw_ready, 1)
                pe.wait_ge(y_ready, L + 1)
                turn(8 + 16 * L, lambda t, k: p1[:, t, GATE + k * P:GATE + (k + 1) * P])
                with pe.Fori(0, 2) as i:
                    for p in range(2):
                        pe.wait_ge(turn_lo, 16 + 16 * L)
                        pe.wait_ge(x_summed, L * 4 + 2 * i + p + 1)
                        for s in range(8):
                            chunk(B0 + AT_OUT + 4 * i + 2 * p, s, of_group(s, (2 * p, 2 * p + 1)))
                pe.wait_ge(x_ready, L + 1)
                turn(16 + 16 * L, lambda t, k: x[:, t, k * P:(k + 1) * P])
                pe.wait_ge(turn_lo, 24 + 16 * L)

            for q in range(TT):
                pe.wait_ge(rpb_landed, 256 * (q + 1))
                for n in range(4):
                    if q:
                        pe.wait_ge(na_biased, n + 1)
                    nc.tensor.matmul(ps[n][:, :], flip, rpb_rows[:, n * 512:(n + 1) * 512], start=True, stop=True)\
                        .then_inc(na_flipped, 1)
            pe.wait_ge(ctx_ready, 1)
            turn(TURN_KVC, lambda t, k: ctx_tok[:, t, k * P:(k + 1) * P])
            pe.wait_ge(turn_lo, TURN_KVC + 8)
            pe.wait_ge(na_biased, 8)
            with pe.Fori(0, 2) as i:
                for p in range(2):
                    for e in (evac_a, evac_d):
                        pe.wait_ge(e, 30 + 2 * i + p + 1)
                    for s in range(8):
                        chunk(AT_KVC + 4 * i + 2 * p, s, of_group(s, (2 * p, 2 * p + 1)))
            pe.wait_ge(xn_ready, 1)
            turn(TURN_H, lambda t, k: xn[:, t, k * P:(k + 1) * P])
            pe.wait_ge(turn_lo, TURN_H + 8)
            with pe.Fori(0, 5) as i:
                for p in range(2):
                    for e in (evac_a, evac_d):
                        pe.wait_ge(e, 34 + 2 * i + p + 1)
                    for s in range(8):
                        chunk(AT_IN2 + 4 * i + 2 * p, s, of_group(s, (2 * p, 2 * p + 1)))
            for e in (evac_a, evac_d):
                pe.wait_ge(e, 44 + 1)
            for s in range(8):
                chunk(AT_IN2 + 20, s, of_group(s, (0, 1)))
            for e in (evac_a, evac_d):
                pe.wait_ge(e, 45 + 2)
            turn_cols((0, 1), lambda t, j: p2[:, t, POOL + j * P:POOL + (j + 1) * P], pool_turned)
            pe.wait_ge(u_ready, 1)
            turn_cols((6, 7), lambda t, j: p2[:, t, SB + j * P:SB + (j + 1) * P])
            turn_cols((4, 5), lambda t, j: p2[:, t, SV + j * P:SV + (j + 1) * P], u_turned)
            pe.wait_ge(pool_ready, 1)
            pe.wait_ge(wp_landed, 16)
            pe.wait_ge(u_copied, 1)
            for g in range(4):
                mm = nc.tensor.matmul(ps[4 + g // 2][:, (g % 2) * S:(g % 2 + 1) * S], p2[:, 0, SV + g * P:SV + (g + 1) * P],
                                      pool_p[:, g, :], start=True, stop=True)
            mm.then_inc(pool_out, 1)

            pe.wait_ge(pool_copied, 1)
            pe.wait_ge(pool_scaled, 1)
            for turn_of in range(3):
                pe.wait_ge(br_ready, turn_of + 1)
                with pe.Fori(0, 2) as i:
                    for s in range(20):
                        n, r = 2 * i + s // 10, s % 10
                        g = 4 * turn_of + n
                        H = 24 + g
                        if r == 0:
                            pe.wait_ge(sig_done, g + 1)
                        if r == 8:
                            pe.wait_ge(gate_added, g + 1)
                        chunk(AT_GATES + 10 * turn_of + 5 * i, s,
                              of_group(r, (0, 1)) if r < 8 else of_group(r - 8, (2, 3), 4, br_hi, br_lo))
                        if turn_of == 2:
                            continue
                        if r == 1:
                            turn_heads(H, 6)
                        if r == 3:
                            pe.wait_ge(qkt_copied, H + 1)
                            for t in range(TT):
                                mm = nc.tensor.matmul(ps[6 + t][:, :], qkt[:, t * P:(t + 1) * P], qkt[:, 256:768], start=True, stop=True)
                            mm.then_inc(scores_ready, 1)
                        if r == 6:
                            pe.wait_ge(exps_ready, H + 1)
                            for t in range(TT):
                                for k in range(4):
                                    at = (k % 2) * S + t * P
                                    mm = nc.tensor.transpose(ps[4 + k // 2][:, at:at + P],
                                                             probs[:, t * 512 + k * P:t * 512 + (k + 1) * P], ident)
                            mm.then_inc(pt_ready, 1)
                        if r == 8:
                            pe.wait_ge(pt_copied, H + 1)
                            for t in range(TT):
                                for k in range(4):
                                    v = p2[:, k, bass.ds(NV + g * HD, HD)] if k < 2 else kvc[:, k - 2, bass.ds(1024 + g * HD, HD)]
                                    mm = nc.tensor.matmul(ps[6][:, t * HD:(t + 1) * HD], na_pt[:, k * S + t * P:k * S + (t + 1) * P], v,
                                                          start=k == 0, stop=k == 3)
                            mm.then_inc(pv_ready, 1)
                if turn_of == 1:
                    pe.wait_ge(dft_landed, 16)
                    pe.wait_ge(head_done, 24 + NA_HEADS)
                    for g in range(4):
                        for t in range(TT):
                            mm = nc.tensor.matmul(ps[4 + g][:, :], p2[:, t, FT + g * P:FT + (g + 1) * P], dft[:, t * 512:(t + 1) * 512],
                                                  start=t == 0, stop=t == TT - 1)
                        mm.then_inc(ft_cols, 1)
                    pe.wait_ge(ft_copied, 4)
                    for g in range(4):
                        a = p2[:, g // 2, NK + (g % 2) * COLS:NK + (g % 2 + 1) * COLS]
                        o = ps[4 + g // 2][:, (g % 2) * S:(g % 2 + 1) * S]
                        nc.tensor.matmul(o, dft[:, 1024:1152], a[:, 0:S], start=True, stop=False)
                        mm = nc.tensor.matmul(o, dft[:, 1152:1280], a[:, S:2 * S], start=False, stop=True)
                    mm.then_inc(ft_ready, 1)
                    for r in range(8):
                        if r >= 2:
                            pe.wait_ge(row_copied, r - 1)
                        pe.wait_ge(diag_ready, r + 1)
                        nc.tensor.matmul(ps[6 + r % 2][:, :], ones[:, :], stage[:, 0:4, :], start=True, stop=True).then_inc(row_ready, 1)
            pe.wait_ge(sig_done, 13)
            pe.wait_ge(gate_added, 13)
            with pe.Fori(0, 2) as i:
                for p in range(2):
                    pe.wait_ge(sig_done, 12 + 2 * i + p)
                    for s in range(8):
                        chunk(AT_GATE0 + 4 * i + 2 * p, s, of_group(s, (2 * p, 2 * p + 1)))
            turn(TURN_NA, lambda t, k: p2[:, t, NQ + k * P:NQ + (k + 1) * P], 4)
            pe.wait_ge(turn_lo, TURN_NA + 4)
            pe.wait_ge(sig_done, 17)
            with pe.Fori(0, 2) as i:
                for s in range(8):
                    p = s // 4
                    if s % 4 == 0:
                        pe.wait_ge(gate_added, 12 + 2 * i + p)
                    chunk(AT_NAP + 2 * i, s, of_group(s % 4, (2 * p, 2 * p + 1), 8))
            pe.wait_ge(gate_added, 17)
            turn(TURN_Y2, lambda t, k: p2[:, t, Y2 + k * P:Y2 + (k + 1) * P])
            pe.wait_ge(turn_lo, TURN_Y2 + 8)
            with pe.Fori(0, 2) as i:
                for p in range(2):
                    pe.wait_ge(x_summed, 8 + 2 * i + p + 1)
                    for s in range(8):
                        chunk(AT_WO + 4 * i + 2 * p, s, of_group(s, (2 * p, 2 * p + 1)))
            pe.wait_ge(h2_ready, 1)
            turn(TURN_H2, lambda t, k: kvc[:, t, k * P:(k + 1) * P])
            pe.wait_ge(turn_lo, TURN_H2 + 8)

            def turn_hidden(f):
                pe.wait_ge(hid_ready, f + 1)
                turn_cols((4, 5), lambda t, j: kvc[:, t, j * P:(j + 1) * P], hid_turned)

            def down(bar, s0, s, f):
                n = s // 2
                if s == 0:
                    pe.wait_ge(hid_lo, f + 1)
                if s % 2 == 0:
                    pe.wait_ge(acc_done, 4 * f + n + 1)
                chunk(bar, s0 + s, of_group(s % 2, (4, 5) if n % 2 else (6, 7), 4, br_hi, br_lo))

            for s in range(16):
                chunk(AT_FF, s, of_group(s % 8, (0, 1) if s < 8 else (2, 3)))
            with pe.Fori(0, FF - 1) as i:
                bar = AT_FF + 4 + 6 * i
                for s in range(24):
                    if s == 0:
                        pe.wait_ge(silu_done, i + 1)
                    if s == 8:
                        pe.wait_ge(hid_ready, i + 1)
                    if s < 16:
                        chunk(bar, s, of_group(s % 8, (0, 1) if s < 8 else (2, 3)))
                    else:
                        down(bar, 16, s - 16, i)
                    if s == 7:
                        pe.wait_ge(acc_done, 4 * i + 2)
                        turn_hidden(i)
            pe.wait_ge(acc_done, 4 * (FF - 1) + 2)
            turn_hidden(FF - 1)
            for s in range(8):
                down(BARS - 2, 0, s, FF - 1)

        @block.vector
        def _(dve):
            ch = Chain(dve, dve_chain)

            def split(bar, s):
                dve.wait_ge(hi_ready, 4 * bar + s + 5)
                j = s % RING
                nc.vector.tensor_tensor(w_lo[:, j, :], raw[:, j, :], w_hi[:, j, :].bitcast(F32), ALU.subtract).then_inc(lo_ready, 1)

            def rest_of(dst, src, hi):
                return nc.vector.tensor_tensor(dst, src, hi.bitcast(F32), ALU.subtract)

            def turn(first, rounds=8):
                for r in range(rounds):
                    dve.wait_ge(turn_hi, first + r + 1)
                    a = slice(2 * r, 2 * r + 2)
                    rest_of(act_lo[:, a, :], ps[4 + r % 4][:, :].rearrange("p (k t) -> p k t", k=2), act_hi[:, a, :])\
                        .then_inc(turn_lo, 1)

            def turn_modulated(first):
                for r in range(8):
                    dve.wait_ge(turn_hi, first + r + 1)
                    a = slice(2 * r, 2 * r + 2)
                    v = gtmp[:, r % 2, :].rearrange("p (k t) -> p k t", k=2)
                    ch.link(nc.vector.tensor_copy(act_hi[:, a, :], v))
                    rest_of(act_lo[:, a, :], v, act_hi[:, a, :]).then_inc(turn_lo, 1)

            for j in range(RING):
                dve.wait_ge(hi_ready, j + 1)
                nc.vector.tensor_tensor(w_lo[:, j, :], raw[:, j, :], w_hi[:, j, :].bitcast(F32), ALU.subtract).then_inc(lo_ready, 1)
            dve.wait_ge(consts_landed, 80)
            pairs = lam_in.rearrange("p (n two d) -> p n two d", two=2, d=64)
            ch.link(nc.vector.tensor_tensor(probs[:, 0:256].rearrange("p (b d) -> p b d", d=64), pairs[:, :, 0, :], pairs[:, :, 1, :], ALU.mult))
            nc.vector.reduce_sum(lam[:, 0:4], probs[:, 0:256].rearrange("p (b d) -> p b d", d=64), AX_X).then_inc(lam_dots, 1)
            for layer in range(DEPTH):
                g = vec["head_gain"][:, layer * HD:(layer + 1) * HD]
                ch.link(nc.vector.tensor_scalar(g, g, 1.0 - LAM_INIT[layer], None, ALU.mult))
            dve.wait_ge(rel_ready, 1)
            nc.vector.tensor_tensor(rvec, ps[0][0:12, 0:384], mask_r, ALU.add).then_inc(rvec_ready, 1)
            dve.wait_ge(csf_ready, 1)
            c2 = csf[:, :].rearrange("p (k c) -> p k c", c=2)
            ch.link(nc.vector.tensor_copy(cs[:, :, 0:2], c2))
            rest_of(cs[:, :, 2:4], c2, cs[:, :, 0:2]).then_inc(cs_ready, 1)
            dve.wait_ge(lam_exp, 1)
            e = lam[:, 4:8].rearrange("p (l two) -> p l two", two=2)
            ch.link(nc.vector.tensor_tensor(small[:, 56:58].rearrange("p (l o) -> p l o", o=1), e[:, :, 1:2], e[:, :, 0:1], ALU.subtract))
            for layer in range(DEPTH):
                ch.link(nc.vector.tensor_scalar(lam[:, layer:layer + 1], small[:, 56 + layer:57 + layer], LAM_INIT[layer], None, ALU.subtract))
            turn(TURN_X0)
            dve.wait_ge(bias_ready, 6)

            def copy_group(bank, dst):
                nc.vector.tensor_copy(dst, ps[bank][:, :]).then_inc(evac_d, 1)

            def biased_scores(bank, at, head_bias, scale):
                nc.vector.scalar_tensor_tensor(probs[:, at:at + 128], ps[bank][:, 0:128], scale, bias_t[:, bass.ds(head_bias + 128, 128)], ALU.mult, ALU.add)
                ch.link(nc.vector.scalar_tensor_tensor(probs[:, at + 128:at + 384], ps[bank][:, 128:384], scale, bias_t[:, bass.ds(head_bias, 256)],
                                                       ALU.mult, ALU.add))

            def row_maxima(parts):
                for i, (a, b) in enumerate(parts):
                    ins = nc.vector.reduce_max(mx[:, i:i + 1], probs[:, a:b], AX_X)
                ch.link(ins)
                n = len(parts)
                nc.vector.tensor_scalar(nm[:, 0:n], mx[:, 0:n], -1.0, None, ALU.mult).then_inc(max_ready, 1)

            def add_mod(M):
                dve.wait_ge(mod_col_ready, M + 1)
                nc.vector.tensor_tensor(mod_t[:, bass.ds(M * 8, 8)], ps[3][:, 0:8], vec["b_mod"][:, bass.ds(M * 8, 8)], ALU.add).then_inc(mod_done, 1)

            def tap(L, k, before):
                dve.wait_ge(conv_tapped, L * CONV + before)
                for j in range(4):
                    ins = nc.vector.scalar_tensor_tensor(conv_acc[:, j, :], conv_pad[:, j, bass.ds(k, S)],
                                                         vec["conv_dw"][:, bass.ds(L * (4 * CONV) + j * CONV + k, 1)], conv_acc[:, j, :],
                                                         ALU.mult, ALU.add)
                ins.then_inc(conv_tapped, 1)

            with dve.Fori(0, DEPTH) as L, ch.loop(L, DEPTH, DVE_LAYER):
                B0 = L * LAYER_BARS
                with dve.Fori(0, 3) as i:
                    for p in range(2):
                        for s in range(8):
                            split(B0 + 4 * i + 2 * p, s)
                        dve.wait_ge(chunk_used, 4 * B0 + 16 * i + 8 * p + 8)
                        copy_group(2 * p + 1, p1[:, 1, bass.ds((2 * i + p) * COLS, COLS)])
                with dve.Fori(0, B_HEADS) as h, ch.loop(h, B_HEADS, DVE_B):
                    H = L * 12 + h
                    for s in range(16):
                        split(B0 + AT_L2 + 4 * h, s)
                        if s == 4:
                            dve.wait_ge(scores_ready, H + 1)
                            biased_scores(5, 0, (A_HEADS + h) * S, HEAD_SCALE)
                            row_maxima([(0, 128), (128, 384)])
                        if s == 8:
                            dve.wait_ge(exps_ready, H + 1)
                            ch.link(nc.vector.reciprocal(recip[:, 0:2], sums[:, 0:2]))
                        if s == 11:
                            dve.wait_ge(pv_ready, H + 1)
                            for t in range(TT):
                                ins = nc.vector.tensor_scalar(p1[:, t, bass.ds(BQ + h * HD, HD)], ps[7][:, t * HD:(t + 1) * HD],
                                                              recip[:, t:t + 1], None, ALU.mult)
                            ins.then_inc(head_done, 1)
                    dve.wait_ge(chunk_used, 4 * B0 + 4 * AT_L2 + 16 * h + 16)
                    copy_group(1, p1[:, 1, bass.ds(AQ + h * COLS, COLS)])
                    add_mod(L * 12 + h)
                for s in range(8):
                    split(B0 + AT_LAST, s)
                    if s == 0:
                        dve.wait_ge(glu_sig, L + 1)
                        nc.vector.tensor_tensor(p1[:, :, CU:CU + D_C], p1[:, :, CU:CU + D_C], p1[:, :, CGLU:CGLU + D_C], ALU.mult)\
                            .then_inc(glu_ready, 1)
                    if s == 2:
                        dve.wait_ge(conv_in, L + 1)
                        k = CONV - 1
                        for j in range(4):
                            ins = nc.vector.tensor_scalar(conv_acc[:, j, :], conv_pad[:, j, k:k + S],
                                                          vec["conv_dw"][:, bass.ds(L * (4 * CONV) + j * CONV + k, 1)],
                                                          vec["conv_b"][:, bass.ds(L * 4 + j, 1)], ALU.mult, ALU.add)
                        ins.then_inc(conv_tapped, 1)
                    if s in (3, 4):
                        tap(L, CONV + 1 - s, s - 2)
                dve.wait_ge(chunk_used, 4 * B0 + 4 * AT_LAST + 8)
                copy_group(1, p1[:, 1, GATE + 3 * COLS:GATE + 4 * COLS])
                with dve.Fori(0, A_HEADS) as h, ch.loop(h, A_HEADS, DVE_A):
                    H = L * 12 + B_HEADS + h
                    for s in range(8):
                        split(B0 + AT_L3 + 2 * h, s)
                        if s < 7:
                            tap(L, 7 * h + s, 7 * h + s + 3)
                        if s == 2:
                            dve.wait_ge(scores_ready, H + 1)
                            biased_scores(5, 0, h * S, A_SCALE)
                            biased_scores(6, 384, h * S, A_SCALE)
                            row_maxima([(0, 128), (128, 384), (384, 512), (512, 768)])
                        if s == 4:
                            dve.wait_ge(exps_ready, H + 1)
                            ch.link(nc.vector.reciprocal(recip[:, 0:4], sums[:, 0:4]))
                            ch.link(nc.vector.tensor_scalar(nlr[:, 0:2], recip[:, 2:4], lam[:, bass.ds(L, 1)], None, ALU.mult))
                            nc.vector.tensor_scalar(probs[:, 384:512], probs[:, 384:512], nlr[:, 0:1], None, ALU.mult)
                            ch.link(nc.vector.tensor_scalar(probs[:, 512:768], probs[:, 512:768], nlr[:, 1:2], None, ALU.mult))
                            nc.vector.scalar_tensor_tensor(probs[:, 0:128], probs[:, 0:128], recip[:, 0:1], probs[:, 384:512], ALU.mult, ALU.add)
                            nc.vector.scalar_tensor_tensor(probs[:, 128:384], probs[:, 128:384], recip[:, 1:2], probs[:, 512:768], ALU.mult, ALU.add)\
                                .then_inc(diff_ready, 1)
                        if s == 6:
                            dve.wait_ge(squares_ready, L * A_HEADS + h + 1)
                            nc.vector.tensor_scalar(ms[:, 0:2], ss[:, 0:2], 1.0 / HD, EPS, ALU.mult, ALU.add).then_inc(ms_ready, 1)
                    dve.wait_ge(rstd_ready, L * 6 + h + 1)
                    for t in range(TT):
                        ins = nc.vector.scalar_tensor_tensor(p1[:, t, bass.ds(AQ + h * HD, HD)], ps[7][:, t * HD:(t + 1) * HD], rstd[:, t:t + 1],
                                                             vec["head_gain"][:, bass.ds(L * HD, HD)], ALU.mult, ALU.mult)
                    ins.then_inc(head_done, 1)
                    add_mod(L * 12 + B_HEADS + h)
                dve.wait_ge(conv_turned, L + 1)
                for t in range(TT):
                    ins = nc.vector.bn_stats(stats[:, t, 0:6], ps[4 + t][:, :])
                ch.link(ins)
                dve.wait_ge(gates_ready, L + 1)
                nc.vector.tensor_tensor(p1[:, :, GATE:GATE + D_A], p1[:, :, GATE:GATE + D_A], p1[:, :, AQ:AQ + D_A], ALU.mult)
                for t in range(TT):
                    ins = nc.vector.bn_aggr(mv[:, t, :], stats[:, t, 0:6])
                ch.link(ins)
                nc.vector.tensor_scalar(ms[:, 0:2], mv[:, 0:2, 1], EPS, None, ALU.add).then_inc(ms_ready, 1)
                dve.wait_ge(rstd_ready, L * 6 + 5)
                for t in range(TT):
                    ins = nc.vector.tensor_scalar(p1[:, t, AK:AK + D_C], ps[4 + t][:, :], mv[:, t, 0:1], rstd[:, t:t + 1], ALU.subtract, ALU.mult)
                ins.then_inc(cn_ready, 1)
                nc.vector.tensor_tensor(p1[:, :, GATE + D_A:GATE + D_A + D_B], p1[:, :, GATE + D_A:GATE + D_A + D_B], p1[:, :, BQ:BQ + D_B], ALU.mult)
                dve.wait_ge(cpw_ready, L + 1)
                for t in range(TT):
                    ins = nc.vector.tensor_tensor(p1[:, t, GATE + D_A + D_B:W1], ps[t][:, :], p1[:, t, GATE + D_A + D_B:W1], ALU.mult)
                ins.then_inc(y_ready, 1)
                turn(8 + 16 * L)
                with dve.Fori(0, 2) as i, ch.loop(i, 2, 2):
                    for p in range(2):
                        n = 2 * i + p
                        for s in range(8):
                            split(B0 + AT_OUT + 4 * i + 2 * p, s)
                        dve.wait_ge(chunk_used, 4 * B0 + 4 * AT_OUT + 16 * i + 8 * p + 8)
                        for t in range(TT):
                            xs = x[:, t, bass.ds(n * COLS, COLS)]
                            ins = nc.vector.scalar_tensor_tensor(xs, xs, ALPHA, ps[2 * p + t][:, :], ALU.mult, ALU.add)
                        ins.then_inc(x_summed, 1)
                        dve.wait_ge(x_summed, L * 4 + n + 3)
                        for t in range(TT):
                            ins = nc.vector.bn_stats(stats[:, t, bass.ds(n * 6, 6)], x[:, t, bass.ds(n * COLS, COLS)])
                        ch.link(ins)
                dve.wait_ge(x_summed, 2)
                for t in range(TT):
                    ins = nc.vector.bn_aggr(mv[:, t, :], stats[:, t, :].rearrange("p (n s) -> p n s", s=6))
                ch.link(ins)
                nc.vector.tensor_scalar(ms[:, 0:2], mv[:, 0:2, 1], EPS, None, ALU.add).then_inc(ms_ready, 1)
                dve.wait_ge(rstd_ready, L * 6 + 6)
                for t in range(TT):
                    ins = nc.vector.tensor_scalar(x[:, t, :], x[:, t, :], mv[:, t, 0:1], rstd[:, t:t + 1], ALU.subtract, ALU.mult)
                ch.link(ins)
                dve.wait_ge(ln_landed, 32 * (L + 1))
                for t in range(TT):
                    ins = nc.vector.tensor_tensor(x[:, t, :], x[:, t, :], p1[:, 0, BK:BK + D], ALU.mult)
                ch.link(ins)
                for t in range(TT):
                    ins = nc.vector.tensor_tensor(x[:, t, :], x[:, t, :], p1[:, 1, BK:BK + D], ALU.add)
                ins.then_inc(x_ready, 1)
                turn(16 + 16 * L)

            dve.wait_ge(mod_done, MOD_GROUPS)
            n1 = vec["norm1"].rearrange("p (k c) -> p k c", c=2)
            nc.vector.scalar_tensor_tensor(hs1[:, :, :], mod3[:, KT:2 * KT, :], 1.0, n1, ALU.add, ALU.mult).then_inc(scale_ready, 1)
            nc.vector.scalar_tensor_tensor(hs2[:, :], mod3[:, 4 * KT:5 * KT, 0], 1.0, vec["norm2"], ALU.add, ALU.mult).then_inc(scale_ready, 1)

            def mean_squares(tiles):
                for i, (t, src) in enumerate(tiles):
                    for n in range(4):
                        ins = nc.vector.bn_stats(stats[:, i, n * 6:n * 6 + 6], src[:, n * COLS:(n + 1) * COLS])
                ch.link(ins)
                n = len(tiles)
                for i in range(n):
                    ins = nc.vector.bn_aggr(mv[:, i, :], stats[:, i, :].rearrange("p (n s) -> p n s", s=6))
                ch.link(ins)
                ch.link(nc.vector.tensor_tensor(ms[:, 0:n], mv[:, 0:n, 0], mv[:, 0:n, 0], ALU.mult))
                nc.vector.scalar_tensor_tensor(ms[:, 0:n], ms[:, 0:n], RMS_EPS, mv[:, 0:n, 1], ALU.add, ALU.add).then_inc(ms_ready, 1)

            dve.wait_ge(ctx_landed, 16)
            mean_squares([(t, ctx_tok[:, t, :]) for t in range(TT)] + [(t, x[:, t, :]) for t in range(TT)])
            dve.wait_ge(rstd_ready, 13)
            for t in range(TT):
                ins = nc.vector.tensor_scalar(ctx_tok[:, t, :], ctx_tok[:, t, :], rstd[:, t:t + 1], None, ALU.mult)
            ins.then_inc(ctx_ready, 1)
            for t in range(TT):
                ins = nc.vector.tensor_scalar(xn[:, t, :], x[:, t, :], rstd[:, 2 + t:3 + t], None, ALU.mult)
            ins.then_inc(xn_ready, 1)
            window = na_mask.rearrange("p (o c) -> p o c", o=1).to_broadcast([P, 8, GRID_W])
            for q in range(TT):
                for n in range(4):
                    dve.wait_ge(na_flipped, 4 * q + n + 1)
                    nc.vector.tensor_tensor(na_bias[:, q, n * 512:(n + 1) * 512].rearrange("p (a c) -> p a c", c=GRID_W),
                                            ps[n][:, :].rearrange("p (a c) -> p a c", c=GRID_W), window, ALU.add).then_inc(na_biased, 1)
            turn_modulated(TURN_KVC)
            with dve.Fori(0, 2) as i:
                for p in range(2):
                    for s in range(8):
                        split(AT_KVC + 4 * i + 2 * p, s)
                    dve.wait_ge(chunk_used, 4 * AT_KVC + 16 * i + 8 * p + 8)
                    copy_group(2 * p + 1, kvc[:, 1, bass.ds((2 * i + p) * COLS, COLS)])
            turn_modulated(TURN_H)
            with dve.Fori(0, 5) as i:
                for p in range(2):
                    for s in range(8):
                        split(AT_IN2 + 4 * i + 2 * p, s)
                    dve.wait_ge(chunk_used, 4 * AT_IN2 + 16 * i + 8 * p + 8)
                    copy_group(2 * p + 1, p2[:, 1, bass.ds((2 * i + p) * COLS, COLS)])
            for s in range(8):
                split(AT_IN2 + 20, s)
            dve.wait_ge(chunk_used, 4 * AT_IN2 + 88)
            copy_group(1, p2[:, 1, SC:SC + COLS])
            dve.wait_ge(evac_a, 47)
            dve.wait_ge(evac_d, 47)
            nc.vector.tensor_tensor(p2[:, :, SV:SV + COLS], p2[:, :, SV:SV + COLS], p2[:, :, SC:SC + COLS], ALU.mult).then_inc(u_ready, 1)
            nc.vector.memset(pool_u[:, :, 0:8], 0.0)
            nc.vector.memset(pool_u[:, :, 264:272], 0.0).then_inc(cleared, 1)
            for i, src in enumerate([p2[:, t, at:at + 1024] for at in (NQ, NK) for t in range(TT)] + [kvc[:, t, 0:1024] for t in range(TT)]):
                ch.link(nc.vector.tensor_tensor(gflat, src, src, ALU.mult))
                ch.link(nc.vector.reduce_sum(ss[:, 8 * i:8 * i + 8], gflat.rearrange("p (h d) -> p h d", d=HD), AX_X))
            nc.vector.tensor_scalar(ms[:, :], ss[:, :], 1.0 / HD, RMS_EPS, ALU.mult, ALU.add).then_inc(ms_ready, 1)
            dve.wait_ge(pool_copied, 1)
            dve.wait_ge(inv_landed, 16)
            for g, w in enumerate(POOL_WINDOWS):
                src, step = pool_u[:, g, :], 0
                for k in range(g + 1):
                    half_w, lo, hi = 2 ** k // 2, 2 ** k, 273 - 2 ** k
                    dst = pool_s[k % 2]
                    a, b = (1, 0) if k == 0 else (half_w, -half_w)
                    ch.link(nc.vector.tensor_tensor(dst[:, lo:hi], src[:, lo - a:hi - a], src[:, lo - b:hi - b], ALU.add))
                    src = dst
                ch.link(nc.vector.tensor_tensor(pool_p[:, g, :], src[:, 8:264], pool_p[:, g, :], ALU.mult))
                ins = nc.vector.tensor_tensor(pool_p[:, g, :], pool_p[:, g, :], pool_u[:, g, 8:264], ALU.subtract)
            ins.then_inc(pool_ready, 1)
            dve.wait_ge(u_copied, 1)
            v = gflat.rearrange("p (j t) -> p j t", j=4)
            w = vec["short_w"]
            for k in range(3):
                for j in range(4):
                    u = conv_pad[:, j, CONV - 2 + k:CONV - 2 + k + S]
                    if k == 0:
                        ins = nc.vector.tensor_scalar(v[:, j, :], u, w[:, 3 * j:3 * j + 1], None, ALU.mult)
                    else:
                        ins = nc.vector.scalar_tensor_tensor(v[:, j, :], u, w[:, 3 * j + k:3 * j + k + 1], v[:, j, :], ALU.mult, ALU.add)
                ch.link(ins)
            for k in range(2):
                ins = nc.vector.tensor_tensor(v[:, 2 * k:2 * k + 2, :], v[:, 2 * k:2 * k + 2, :], ps[6 + k][:, :].rearrange("p (j t) -> p j t", j=2), ALU.mult)
            ch.link(ins)
            ch.link(nc.vector.tensor_copy(br_hi[:, :, :], v))
            rest_of(br_lo[:, :, :], v, br_hi[:, :, :]).then_inc(br_ready, 1)

            for turn_of in range(3):
                if turn_of == 1:
                    dve.wait_ge(pool_scaled, 1)
                    ch.link(nc.vector.tensor_copy(br_hi[:, :, :], pool_v))
                    rest_of(br_lo[:, :, :], pool_v, br_hi[:, :, :]).then_inc(br_ready, 1)
                if turn_of == 2:
                    dve.wait_ge(ft_ready, 1)
                    f = [ps[4 + k][:, :].rearrange("p (j t) -> p j t", j=2) for k in range(2)]
                    for k in range(2):
                        ins = nc.vector.tensor_copy(br_hi[:, 2 * k:2 * k + 2, :], f[k])
                    ch.link(ins)
                    for k in range(2):
                        ins = rest_of(br_lo[:, 2 * k:2 * k + 2, :], f[k], br_hi[:, 2 * k:2 * k + 2, :])
                    ins.then_inc(br_ready, 1)
                    for r in range(8):
                        if r:
                            dve.wait_ge(row_ready, r)
                        for j in range(4):
                            at = (2, 5)[r // 4] * KT + (r % 4) * 4 + j
                            ins = nc.vector.tensor_scalar(stage[:, j, :], ident, mod3[:, at, 0:1], None, ALU.mult)
                        ins.then_inc(diag_ready, 1)
                with dve.Fori(0, 2) as i, ch.loop(i, 2, DVE_GATES[turn_of]):
                    for s in range(20):
                        n, r = 2 * i + s // 10, s % 10
                        g = 4 * turn_of + n
                        H = 24 + g
                        split(AT_GATES + 10 * turn_of + 5 * i, s)
                        if r == 9:
                            dve.wait_ge(sig_done, g + 2)
                            dve.wait_ge(chunk_used, 4 * AT_GATES + 40 * turn_of + 20 * i + s + 1)
                            for t in range(TT):
                                y = p2[:, t, bass.ds(Y2 + n * COLS, COLS)]
                                ins = nc.vector.tensor_tensor(y if turn_of == 0 else gtmp[:, t, :], gtmp[:, t, :], ps[2 + t][:, :], ALU.mult)
                            if turn_of:
                                ch.link(ins)
                                for t in range(TT):
                                    y = p2[:, t, bass.ds(Y2 + n * COLS, COLS)]
                                    ins = nc.vector.tensor_tensor(y, y, gtmp[:, t, :], ALU.add)
                            ins.then_inc(gate_added, 1)
                        if turn_of == 2:
                            continue
                        if r == 3:
                            dve.wait_ge(scores_ready, H + 1)
                            for t in range(TT):
                                nc.vector.scalar_tensor_tensor(probs[:, t * 512:t * 512 + 256], ps[6 + t][:, 0:256], HEAD_SCALE,
                                                               na_bias[:, t, bass.ds(g * 256, 256)], ALU.mult, ALU.add)
                                ins = nc.vector.tensor_scalar(probs[:, t * 512 + 256:t * 512 + 512], ps[6 + t][:, 256:512], HEAD_SCALE, None, ALU.mult)
                            ch.link(ins)
                            row_maxima([(0, 512), (512, 1024)])
                        if r == 6:
                            dve.wait_ge(exps_ready, H + 1)
                            ch.link(nc.vector.reciprocal(recip[:, 0:2], sums[:, 0:2]))
                        if r == 8:
                            dve.wait_ge(pv_ready, H + 1)
                            for t in range(TT):
                                ins = nc.vector.tensor_scalar(p2[:, t, bass.ds(NQ + g * HD, HD)], ps[6][:, t * HD:(t + 1) * HD],
                                                              recip[:, t:t + 1], None, ALU.mult)
                            ins.then_inc(head_done, 1)
            with dve.Fori(0, 2) as i:
                for p in range(2):
                    for s in range(8):
                        split(AT_GATE0 + 4 * i + 2 * p, s)
            turn(TURN_NA, 4)
            with dve.Fori(0, 2) as i, ch.loop(i, 2, 2):
                for s in range(8):
                    p = s // 4
                    split(AT_NAP + 2 * i, s)
                    if s % 4 == 3:
                        dve.wait_ge(sig_done, 17)
                        dve.wait_ge(chunk_used, 4 * AT_NAP + 8 * i + s + 1)
                        dve.wait_ge(gate_added, 13 + 2 * i + p)
                        for t in range(TT):
                            ins = nc.vector.tensor_tensor(gtmp[:, t, :], kvc[:, t, bass.ds((2 * i + p) * COLS, COLS)], ps[2 * p + t][:, :], ALU.mult)
                        ch.link(ins)
                        for t in range(TT):
                            y = p2[:, t, bass.ds(Y2 + (2 * i + p) * COLS, COLS)]
                            ins = nc.vector.tensor_tensor(y, y, gtmp[:, t, :], ALU.add)
                        ins.then_inc(gate_added, 1)
            turn(TURN_Y2)
            with dve.Fori(0, 2) as i, ch.loop(i, 2, 2):
                for p in range(2):
                    n = 2 * i + p
                    for s in range(8):
                        split(AT_WO + 4 * i + 2 * p, s)
                    dve.wait_ge(chunk_used, 4 * AT_WO + 16 * i + 8 * p + 8)
                    dve.wait_ge(x_summed, 2 + 4 * DEPTH + n)
                    dve.wait_ge(row_copied, 8)
                    for t in range(TT):
                        ins = nc.vector.tensor_tensor(gtmp[:, t, :], ps[2 * p + t][:, :], flat[:, bass.ds(i * W2 + NV + p * COLS, COLS)], ALU.mult)
                    ch.link(ins)
                    for t in range(TT):
                        xs = x[:, t, bass.ds(n * COLS, COLS)]
                        ins = nc.vector.tensor_tensor(xs, xs, gtmp[:, t, :], ALU.add)
                    ins.then_inc(x_summed, 1)
            dve.wait_ge(x_summed, 2 + 4 * DEPTH + 4)
            mean_squares([(t, x[:, t, :]) for t in range(TT)])
            dve.wait_ge(rstd_ready, 15)
            for t in range(TT):
                ins = nc.vector.tensor_scalar(kvc[:, t, :], x[:, t, :], rstd[:, t:t + 1], None, ALU.mult)
            ins.then_inc(h2_ready, 1)
            ch.link(nc.vector.memset(p2[:, :, Y2:Y2 + D], 0.0))
            turn_modulated(TURN_H2)

            def hidden(f):
                dve.wait_ge(silu_done, f + 1)
                for t in range(TT):
                    ins = nc.vector.tensor_tensor(kvc[:, t, 0:COLS], gtmp[:, t, :], ps[2 + t][:, :], ALU.mult)
                ins.then_inc(hid_ready, 1)

            def hidden_lo(f):
                dve.wait_ge(hid_hi, f + 1)
                for k in range(2):
                    ins = rest_of(br_lo[:, 2 * k:2 * k + 2, :], ps[4 + k][:, :].rearrange("p (j t) -> p j t", j=2), br_hi[:, 2 * k:2 * k + 2, :])
                ins.then_inc(hid_lo, 1)

            for s in range(16):
                split(AT_FF, s)
            dve.wait_ge(chunk_used, 4 * AT_FF + 16)
            hidden(0)
            with dve.Fori(0, FF - 1) as i:
                for s in range(24):
                    split(AT_FF + 4 + 6 * i, s)
                    if s == 7:
                        hidden_lo(i)
                    if s == 15:
                        dve.wait_ge(chunk_used, 4 * AT_FF + 16 + 24 * i + 16)
                        hidden(i + 1)
                    if s >= 16 and s % 2:
                        dve.wait_ge(chunk_used, 4 * AT_FF + 16 + 24 * i + s + 1)
                        dve.wait_ge(acc_done, 2)
                        for t in range(TT):
                            n = (s - 16) // 2
                            acc = p2[:, t, Y2 + n * COLS:Y2 + (n + 1) * COLS]
                            ins = nc.vector.tensor_tensor(acc, acc, ps[((4, 5) if n % 2 else (6, 7))[t]][:, :], ALU.add)
                        ins.then_inc(acc_done, 1)
            hidden_lo(FF - 1)
            for s in range(8):
                if s < 4:
                    split(BARS - 2, s)
                if s % 2:
                    n = s // 2
                    dve.wait_ge(chunk_used, 4 * BARS - 8 + s + 1)
                    for t in range(TT):
                        acc = p2[:, t, Y2 + n * COLS:Y2 + (n + 1) * COLS]
                        ins = nc.vector.tensor_tensor(acc, acc, ps[((4, 5) if n % 2 else (6, 7))[t]][:, :], ALU.add)
                    ins.then_inc(acc_done, 1)
            dve.wait_ge(acc_done, 4 * FF + 2)
            for t in range(TT):
                for k in range(2):
                    acc = p2[:, t, Y2 + k * 1024:Y2 + (k + 1) * 1024]
                    ins = nc.vector.tensor_tensor(acc, acc, p2[:, k, NK:NK + 1024], ALU.mult)
                ch.link(ins)
                nc.vector.tensor_tensor(x[:, t, :], x[:, t, :], p2[:, t, Y2:Y2 + D], ALU.add).then_inc(out_ready, 1)


def position_bucket(d):
    exact = N_BUCKETS // 2
    df = np.maximum(d, 1).astype(np.float32)
    large = exact + (np.log(df / np.float32(exact)) / np.float32(math.log(MAX_DISTANCE / exact)) * np.float32(N_BUCKETS - exact)).astype(np.int32)
    return np.where(d < exact, d, np.minimum(large, N_BUCKETS - 1))


def shape_constants():
    consts = np.zeros((P + N_BUCKETS + A_HEADS + B_HEADS, 384), np.float32)
    consts[0:P, 0:128] = np.eye(P)
    consts[0:P, 128:256] = np.eye(P)[::-1]
    j, c = np.arange(P) % GRID_W, np.arange(GRID_W)
    first = np.clip(j - NA_KW // 2, 0, GRID_W - NA_KW)[:, None]
    consts[0:P, 256:320] = np.where((c >= first) & (c < first + NA_KW), 0.0, MASKED)
    consts[[0, 1, 2, 3], [320, 321, 320, 321]] = 1.0
    d = S - 1 - np.arange(384)
    seen = d >= 0
    consts[P + position_bucket(np.maximum(d, 0))[seen], np.arange(384)[seen]] = 1.0
    times = seen * ((d <= 128).astype(int) + (d % 4 == 0) + (d % 16 == 0))
    at = P + N_BUCKETS
    consts[at:at + A_HEADS] = np.where(seen, 0.0, MASKED)
    consts[at + A_HEADS:at + A_HEADS + B_HEADS] = np.where(times > 0, np.log(np.maximum(times, 1)), MASKED)
    pos, ch = np.outer(np.arange(S), np.arange(S)) * (2 * np.pi / S), np.outer(np.arange(P), np.arange(P)) * (2 * np.pi / P)
    norm = 1.0 / math.sqrt(S * P)
    rows = np.concatenate([np.cos(pos), np.sin(pos)], axis=1).reshape(TT, P, 2 * S)
    dft = np.concatenate([rows[0], rows[1], np.cos(ch) * norm, -np.sin(ch) * norm], axis=1).astype(np.float32)
    t = np.arange(S)
    inv = np.stack([1.0 / (np.clip(t - w // 2 + w, 0, S) - np.clip(t - w // 2, 0, S)) for w in POOL_WINDOWS])
    inv = np.broadcast_to(inv.astype(np.float32), (P, 4, S))
    return consts, np.ascontiguousarray(dft), np.ascontiguousarray(inv)


def weight_stream(a):
    stream = np.empty((BARS, P, TILES_PER_BAR, COLS), np.float32)
    at = 0

    def put(w, row, col):
        nonlocal at
        stream[at // TILES_PER_BAR, :, at % TILES_PER_BAR, :] = w[row * P:(row + 1) * P, col * COLS:(col + 1) * COLS]
        at += 1

    def put_group(w, col, k0=0, k1=None):
        for k in range(k0, w.shape[0] // P if k1 is None else k1):
            put(w, k, col)

    w_mod = a["w_mod_2"][0]
    order = [4, 5, 6, 7, 8, 9, 0, 1, 2, 12, 13, 3, 10, 11, 14]
    for layer in range(DEPTH):
        w = a["w_in"][layer]
        for g in order[:6]:
            put_group(w, g)
        for h in range(B_HEADS):
            for k in range(KT // 2):
                put_group(w_mod, layer * 12 + h, 2 * k, 2 * k + 2)
                put_group(w, order[6 + h], 2 * k, 2 * k + 2)
        put_group(w, order[14])
        for h in range(A_HEADS):
            put_group(w_mod, layer * 12 + B_HEADS + h)
        for g in range(D // COLS):
            put_group(a["w_out"][layer], g)
    w = a["w_in_2"][0]
    for g in (2, 3, 4, 5):
        put_group(w, g)
    for g in range(11):
        put_group(w, g)
    gates = a["w_gate_2"][0]
    for i, branch in ((3, "w_pd_2"), (2, "w_pc_2"), (1, "w_pb_2")):
        for g in range(D // COLS):
            put_group(gates[i], g)
            put_group(a[branch][0], g)
    for w in (gates[0], a["w_pa_2"][0], a["w_o_2"][0]):
        for g in range(D // COLS):
            put_group(w, g)
    w_gate, w_up, w_down = (a[f"w_ffn_{n}_2"][0] for n in ("gate", "up", "down"))
    for f in range(FF + 1):
        if f < FF:
            put_group(w_gate, f)
            put_group(w_up, f)
        if f:
            for g in range(D // COLS):
                put_group(w_down, g, 4 * (f - 1), 4 * f)
    assert at == BARS * TILES_PER_BAR
    return stream.reshape(BARS, P, TILES_PER_BAR * COLS)


def columns(v, n):
    return v.reshape(n, P).T


def parameter_vectors(a):
    twice = lambda v: np.repeat(v[:, :, None], 2, axis=2).reshape(P, -1)
    per_layer = lambda v: np.concatenate([columns(v[layer], 4) for layer in range(DEPTH)], axis=1)
    rel = np.zeros((P, A_HEADS + B_HEADS), np.float32)
    rel[0:N_BUCKETS] = a["rel_bias"]
    dw = a["conv_dw"].reshape(DEPTH, CONV, 4, P).transpose(3, 0, 2, 1).reshape(P, -1)
    parts = {
        "c_cols": np.stack([columns(a["c_2"][0], KT), columns(a["c_ctx_2"], KT)], axis=2).reshape(P, -1),
        "b_mod": twice(columns(a["b_mod_2"][0], N_MOD * KT)),
        "rel_bias": rel,
        "head_gain": np.broadcast_to(a["diff_head_gain"].reshape(1, -1), (P, DEPTH * HD)),
        "conv_dw": dw,
        "conv_b": per_layer(a["conv_b"]), "conv_g": per_layer(a["conv_ln_g"]), "conv_beta": per_layer(a["conv_ln_b"]),
        "norm1": twice(columns(a["norm1_w_2"][0], KT)),
        "norm2": columns(a["norm2_w_2"][0], KT),
        "q_norm": a["q_norm_w_2"].reshape(P, 1), "k_norm": a["k_norm_w_2"].reshape(P, 1),
        "pool_scale": columns(a["pool_scale_2"][0], 4),
        "short_w": a["conv_w_2"][0].reshape(3, 4, P).transpose(2, 1, 0).reshape(P, -1),
    }
    assert all(parts[n].shape == (P, w) for n, w in VECS), [(n, parts[n].shape) for n, _ in VECS]
    return np.ascontiguousarray(np.concatenate([parts[n] for n, _ in VECS], axis=1))


def kernel(**inputs):
    import concourse.bacc as bacc
    from concourse.bass_utils import run_bass_kernel_spmd

    a = {k: np.asarray(v) for k, v in inputs.items()}
    consts, dft, inv = shape_constants()
    arrays = {
        "weights": weight_stream(a),
        "x_in": np.ascontiguousarray(a["x"].reshape(S, D)),
        "consts": consts,
        "vecs": parameter_vectors(a),
        "lam_rows": np.ascontiguousarray(a["diff_lambda"].reshape(1, -1)),
        "rpb": np.ascontiguousarray(a["rpb_2"].reshape(NA_HEADS, RPB_H * RPB_W)),
        "ctx_in": np.ascontiguousarray(a["ctx_2"].reshape(S, D)),
        "ln_gb": np.ascontiguousarray(np.stack([a["ln_g"], a["ln_b"]], axis=1)),
        "conv_pw": np.ascontiguousarray(a["conv_pw"].reshape(DEPTH * 4, P, COLS)),
        "cs_dft": dft,
        "inv_cnt": inv,
        "w_pool": np.ascontiguousarray(a["w_pool_2"][0].transpose(1, 0, 2).reshape(P, 4 * P)),
    }
    nc = bacc.Bacc("TRN2", target_bir_lowering=False, num_devices=1)
    args = [nc.dram_tensor(n, v.shape, F32, kind="ExternalInput").ap() for n, v in arrays.items()]
    scratch = nc.dram_tensor("scratch", (A_HEADS + B_HEADS, 384), F32, kind="Internal").ap()
    out = nc.dram_tensor("out", (S, D), F32, kind="ExternalOutput").ap()
    build(nc, *args, scratch, out)
    r = run_bass_kernel_spmd(nc, [arrays], core_ids=[0])
    return r.results[0]["out"].reshape(1, S, D)
```

```python
import math
from contextlib import ExitStack, contextmanager

import numpy as np

import concourse.bass as bass
from concourse import mybir

F32 = mybir.dt.float32
F32R = mybir.dt.float32r
ALU = mybir.AluOpType
ACT = mybir.ActivationFunctionType
AX_X = mybir.AxisListType.X

P = 128
D = 2048
S = 256
TT = S // P
KT = D // P
COLS = 512
DEPTH = 2
A_HEADS, B_HEADS, NA_HEADS = 4, 8, 8
HD = 128
D_A, D_B, D_C = A_HEADS * HD, B_HEADS * HD, 512
CONV = 31
N_BUCKETS, MAX_DISTANCE = 32, 2048
ALPHA = (2 * DEPTH) ** 0.25
EPS, RMS_EPS = 1e-5, 1e-6
A_SCALE, HEAD_SCALE = (HD // 2) ** -0.5, HD ** -0.5
LAM_INIT = [0.8 - 0.6 * math.exp(-0.3 * layer) for layer in range(DEPTH)]
MASKED = -1.0e30
GRID_W, NA_KW, RPB_H, RPB_W = 64, 16, 15, 31
D_FF = 5632
FF = D_FF // COLS
N_MOD = 6
MOD_GROUPS = N_MOD * D // COLS
POOL_WINDOWS = (2, 4, 8, 16)

RING = 4
TILES_PER_BAR = 8
GROUPS_1 = 15
L1_BARS, GLU_BARS, L2_BARS, L3_BARS, OUT_BARS = 8, 2, 32, 12, 8
LAYER_BARS = L1_BARS + GLU_BARS + L2_BARS + L3_BARS + OUT_BARS
AT_GLU = L1_BARS
AT_L2 = AT_GLU + GLU_BARS
AT_L3 = AT_L2 + L2_BARS
AT_OUT = AT_L3 + L3_BARS
AT_KVC = DEPTH * LAYER_BARS
AT_IN2 = AT_KVC + 8
AT_GATES = AT_IN2 + 22
AT_GATE0 = AT_GATES + 30
AT_NAP = AT_GATE0 + 8
AT_WO = AT_NAP + 4
AT_FF = AT_WO + 8
BARS = AT_FF + 6 * FF

CU, CGLU, BQ, BK, BV, AQ, AK, AV, GATE = 0, 512, 1024, 1536, 2048, 4096, 4608, 5120, 5632
GATE_B, GATE_A, GATE_C = GATE, GATE + D_B, GATE + D_B + D_A
B_HALF = 3 * COLS
W1 = GROUPS_1 * COLS
NQ, NK, NV, POOL, SV, SB, SC, FT = 0, 1024, 2048, 3072, 3584, 4096, 4608, 5120
W2 = 11 * COLS
Y2 = POOL


DVE_B, DVE_A, DVE_GATES, DVE_LAYER = 3, 12, (6, 8, 2), 59

TURN_BANKS, Y_BANKS = (4, 5, 6, 7), (2, 0, 1, 3, 2, 3, 4, 5)

MIX = [("mod", 0)] + [m for k in range(7) for m in (("mod", k + 1), ("group", k))] + [("group", 7)]

VECS = (("c_cols", 2 * KT), ("b_mod", 2 * N_MOD * KT), ("rel_bias", A_HEADS + B_HEADS), ("head_gain", DEPTH * HD),
        ("conv_dw", DEPTH * 4 * CONV), ("conv_b", DEPTH * 4), ("conv_g", DEPTH * 4), ("conv_beta", DEPTH * 4),
        ("norm1", 2 * KT), ("norm2", KT), ("q_norm", 1), ("k_norm", 1), ("pool_scale", 4), ("short_w", 12))


class Chain:

    def __init__(self, eng, sem):
        self.eng, self.sem, self.base, self.n = eng, sem, 0, 0

    def link(self, ins):
        ins.then_inc(self.sem, 1)
        self.n += 1
        self.eng.wait_ge(self.sem, self.base + self.n)

    @contextmanager
    def loop(self, i, rounds, steps):
        base, n = self.base, self.n
        self.base, self.n = i * steps + n + base, 0
        yield
        assert self.n == steps, (self.n, steps)
        self.base, self.n = base, n + rounds * steps


def build(nc, stream, x_in, consts, vecs, lam_rows, rpb, ctx_in, ln_gb, conv_pw, cs_dft, inv_cnt, w_pool, scratch, out):
    with ExitStack() as ctx:
        def sb(name, shape, dt=F32):
            return ctx.enter_context(nc.sbuf_tensor(name, shape, dt))

        def sem(name):
            return ctx.enter_context(nc.semaphore(name))

        raw = sb("raw", [P, RING, 2 * COLS])
        w_hi = sb("w_hi", [P, RING, 2 * COLS], F32R)
        w_lo = sb("w_lo", [P, RING, 2 * COLS], F32R)
        act_hi = sb("act_hi", [P, KT, S], F32R)
        act_lo = sb("act_lo", [P, KT, S], F32R)
        br_hi = sb("br_hi", [P, 4, S], F32R)
        br_lo = sb("br_lo", [P, 4, S], F32R)
        cs_flat = sb("cs", [P, 4 * KT + P - 4], F32R)
        cs = cs_flat[:, 0:4 * KT].rearrange("p (k c) -> p k c", c=4)
        x = sb("x", [P, TT, D])
        flat = sb("flat", [P, TT * W1])
        p1 = flat[:, :].rearrange("p (t c) -> p t c", t=TT)
        p2 = flat[:, 0:TT * W2].rearrange("p (t c) -> p t c", t=TT)
        kvc = flat[:, TT * W2:TT * W1].rearrange("p (t c) -> p t c", t=TT)
        ln_rows = [p1[:, n, BK:BK + 2 * B_HALF].rearrange("p (h c) -> p h c", h=2)[:, :, 0:1024] for n in range(2)]
        ctx_tok = p1[:, :, AQ:AQ + D]
        xn = flat[:, 0:TT * D].rearrange("p (t c) -> p t c", t=TT)
        rpb_rows = flat[:, 2 * TT * D:2 * TT * D + 2048]
        shared = sb("shared", [P, 4096])
        bias_t = shared[:, 0:3072]
        conv_acc = shared[:, 3072:4096].rearrange("p (j t) -> p j t", j=4)
        na_bias = shared[:, :].rearrange("p (q n) -> p q n", q=TT)
        dft = shared[:, 0:1280]
        head = sb("head", [P, 2688])
        stage = head[:, 0:768].rearrange("p (i d) -> p i d", d=HD)
        qkt = head[:, 768:1536]
        probs = head[:, 1536:2560]
        p_t = head[:, 2304:2688]
        na_pt = head[:, 0:1024]
        diag = head[:, 0:2048].rearrange("p (r c) -> p r c", c=COLS)
        ft_by_pos = diag
        pool_u = head[:, 0:1088].rearrange("p (g t) -> p g t", g=4)
        pool_p = head[:, 1088:2112].rearrange("p (g t) -> p g t", g=4)
        pool_s = [head[:, 2112 + 272 * i:2112 + 272 * (i + 1)] for i in range(2)]
        gtmp = sb("gtmp", [P, TT, COLS])
        gflat = gtmp[:, :, :].rearrange("p t c -> p (t c)")
        mod_row = gtmp[0:4, 0, :]
        junk = gtmp[:, 1, :].rearrange("p (t d) -> p t d", d=HD)
        lam_in = gtmp[:, 1, :]
        conv_pad = sb("conv_pad", [P, 4, 288])
        early_diag = conv_pad[:, :, :].rearrange("p j t -> p (j t)")[:, 0:1024].rearrange("p (r c) -> p r c", c=COLS)
        pool_v = conv_pad[:, :, :].rearrange("p j t -> p (j t)")[:, 0:1024].rearrange("p (j t) -> p j t", j=4)
        C = sb("consts_sb", [P, consts.shape[1]])
        V = sb("vecs_sb", [P, vecs.shape[1]])
        mod_t = sb("mod_t", [P, 2 * N_MOD * KT])
        mod3 = mod_t[:, :].rearrange("p (n c) -> p n c", c=2)
        hs1 = sb("hs1", [P, KT, 2])
        hs2 = sb("hs2", [P, KT])
        csf = sb("csf", [P, KT * 2])
        lam = sb("lam", [P, 8])
        small = sb("small", [P, 64])
        stats = sb("stats", [P, 4, 4 * 6])
        mv = sb("mv", [P, 4, 2])
        ms = sb("ms", [P, 48])
        rstd = sb("rstd", [P, 48])
        half = sb("half", [P, 48])
        ss = sb("ss", [P, 48])
        ones = sb("ones", [P, P])
        nm, sums, recip, nlr, mx = (small[:, 8 * i:8 * i + 4] for i in range(5))

        ident, flip = C[:, 0:128], C[:, 128:256]
        na_mask = C[:, 256:320]
        comb = C[0:4, 320:322]
        onehot, mask_r = gtmp[0:N_BUCKETS, 0, 0:384], head[0:12, 0:384]
        rvec = head[0:12, 384:768]
        o = 0
        vec = {}
        for name, n in VECS:
            vec[name] = V[:, o:o + n]
            o += n

        ps = [ctx.enter_context(nc.psum_tensor(f"ps{i}", [P, COLS], F32)) for i in range(8)]

        landed = [sem(f"landed{i}") for i in range(RING)]
        hi_ready, lo_ready = sem("hi_ready"), sem("lo_ready")
        chunk_used = sem("chunk_used")
        x_landed, consts_landed = sem("x_landed"), sem("consts_landed")
        rel_ready, rvec_ready, rvec_stored, rows_landed = sem("rel_ready"), sem("rvec_ready"), sem("rvec_stored"), sem("rows_landed")
        rows_flipped, bias_ready = sem("rows_flipped"), sem("bias_ready")
        csf_ready, cs_ready, lam_dots, lam_exp = sem("csf_ready"), sem("cs_ready"), sem("lam_dots"), sem("lam_exp")
        cleared = sem("cleared")
        turned, turn_hi, turn_lo = sem("turned"), sem("turn_hi"), sem("turn_lo")
        evac_a, evac_d = sem("evac_a"), sem("evac_d")
        qk_staged, qkt_ready, qkt_copied = sem("qk_staged"), sem("qkt_ready"), sem("qkt_copied")
        scores_ready, max_ready, exps_ready = sem("scores_ready"), sem("max_ready"), sem("exps_ready")
        diff_ready, pt_ready, pt_copied = sem("diff_ready"), sem("pt_ready"), sem("pt_copied")
        pv_ready, squares_ready, head_done = sem("pv_ready"), sem("squares_ready"), sem("head_done")
        mod_row_ready, mod_col_ready, mod_done = sem("mod_row_ready"), sem("mod_col_ready"), sem("mod_done")
        ms_ready, rstd_ready = sem("ms_ready"), sem("rstd_ready")
        conv_tapped = sem("conv_tapped")
        glu_sig, glu_ready, cu_turned, conv_in = sem("glu_sig"), sem("glu_ready"), sem("cu_turned"), sem("conv_in")
        b_gates_ready, b_gated = sem("b_gates_ready"), sem("b_gated")
        gates_ready, conv_turned, cn_ready = sem("gates_ready"), sem("conv_turned"), sem("cn_ready")
        cn_turned, conv_act, cpw_landed, cpw_ready = sem("cn_turned"), sem("conv_act"), sem("cpw_landed"), sem("cpw_ready")
        a_gated, y_ready, ln_landed, x_ready = sem("a_gated"), sem("y_ready"), sem("ln_landed"), sem("x_ready")
        x_summed = sem("x_summed")
        ctx_landed, rpb_landed, na_flipped, na_biased = sem("ctx_landed"), sem("rpb_landed"), sem("na_flipped"), sem("na_biased")
        scale_ready, ctx_ready, xn_ready = sem("scale_ready"), sem("ctx_ready"), sem("xn_ready")
        u_ready, u_turned, u_copied, pool_turned, pool_copied = sem("u_ready"), sem("u_turned"), sem("u_copied"), sem("pool_turned"), sem("pool_copied")
        inv_landed, wp_landed, pool_ready, pool_out, pool_scaled = sem("inv_landed"), sem("wp_landed"), sem("pool_ready"), sem("pool_out"), sem("pool_scaled")
        u_used = sem("u_used")
        br_ready = sem("br_ready")
        sig_done, gate_added = sem("sig_done"), sem("gate_added")
        dft_landed, ft_cols, ft_copied, ft_ready = sem("dft_landed"), sem("ft_cols"), sem("ft_copied"), sem("ft_ready")
        diag_ready, row_ready, row_copied = sem("diag_ready"), sem("row_ready"), sem("row_copied")
        h2_ready = sem("h2_ready")
        silu_done, hid_ready, hid_turned, hid_hi, hid_lo = sem("silu_done"), sem("hid_ready"), sem("hid_turned"), sem("hid_hi"), sem("hid_lo")
        acc_done = sem("acc_done")
        out_ready, stored = sem("out_ready"), sem("stored")
        dve_chain = sem("dve_chain")

        TURN_X0, TURN_KVC = 0, 8 + 16 * DEPTH
        TURN_H, TURN_NA = TURN_KVC + 8, TURN_KVC + 16
        TURN_Y2, TURN_H2 = TURN_NA + 4, TURN_NA + 12

        block = ctx.enter_context(nc.Block())

        @block.sync
        def _(sp):
            sp.wait_ge(consts_landed, 80)
            sp.dma_start(x[:, :, :], x_in.rearrange("(t p) d -> p t d", p=P)).then_inc(x_landed, 16)
            sp.wait_ge(rvec_stored, 16)
            sp.dma_start(flat[:, 0:3072].rearrange("p (h c) -> p h c", h=12),
                         bass.AP(scratch.tensor, 0, [[1, P], [384, 12], [1, S]])).then_inc(rows_landed, 16)
            for j in range(RING):
                sp.dma_start(raw[:, j, :], stream[0, :, j * 1024:(j + 1) * 1024]).then_inc(landed[j], 16)
            with sp.Fori(1, BARS) as bar:
                for j in range(RING):
                    sp.wait_ge(lo_ready, 4 * bar + j - 3)
                    sp.wait_ge(x_landed, 16)
                    sp.dma_start(raw[:, j, :], stream[bass.ds(bar, 1), :, j * 1024:(j + 1) * 1024])\
                        .then_inc(landed[j], 16)
            for n in range(D // COLS):
                cols = slice(n * COLS, (n + 1) * COLS)
                sp.wait_ge(out_ready, n + 1)
                sp.dma_start(out[:, cols].rearrange("(t p) c -> p t c", p=P), x[:, :, cols]).then_inc(stored, 16)
            sp.wait_ge(stored, 16 * (D // COLS))

        @block.gpsimd
        def _(pool):
            pool.memset(half[:, :], -0.5).then_inc(cleared, 1)
            pool.memset(conv_pad[:, :, :], 0.0).then_inc(cleared, 1)
            pool.memset(ones[:, :], 1.0).then_inc(cleared, 1)
            for k, (count, start) in enumerate(((evac_a, 2), (evac_d, 2), (x_summed, 2), (acc_done, 2), (sig_done, 1), (gate_added, 1))):
                pool.memset(small[:, 48 + k:49 + k], 0.0).then_inc(count, start)
            pool.wait_ge(cleared, 3)

            def inverse_root(index, cols):
                pool.wait_ge(ms_ready, index + 1)
                pool.tensor_tensor(rstd[:, 0:cols], ms[:, 0:cols], half[:, 0:cols], ALU.pow).then_inc(rstd_ready, 1)

            with pool.Fori(0, DEPTH) as L:
                pool.wait_ge(head_done, L * 12 + B_HEADS)
                pool.wait_ge(cleared, 3)
                for t in range(2):
                    row = bass.AP(ln_gb.tensor, L * (2 * D) + t * D, [[0, P], [D // 2, 2], [1, D // 2]])
                    pool.dma_start(ln_rows[t], row).then_inc(ln_landed, 16)
                pool.wait_ge(cu_turned, L + 1)
                pool.wait_ge(cleared, 3)
                for j in range(4):
                    at = CU + (j % 2) * COLS
                    pool.dma_start(p1[:, j // 2, at:at + COLS],
                                   conv_pw[bass.ds(L * 4 + j, 1), :, :]).then_inc(cpw_landed, 16)
                with pool.Fori(0, A_HEADS) as h:
                    inverse_root(L * 6 + h, 2)
                inverse_root(L * 6 + 4, 2)
                inverse_root(L * 6 + 5, 4)

            pool.wait_ge(turn_lo, TURN_KVC)
            inverse_root(12, 2)
            for q in range(TT):
                if q:
                    pool.wait_ge(na_flipped, 4)
                for r in range(2):
                    half_rows = rpb_rows[P - 64 * (r + 1):P - 64 * r, :]
                    with pool.Fori(0, NA_HEADS) as h:
                        src = bass.AP(rpb.tensor, h * (RPB_H * RPB_W) + (7 - 2 * q - r) * RPB_W - 48,
                                      [[1, 64], [RPB_W, 4], [1, GRID_W]])
                        dst = half_rows[:, bass.ds(h * 256, 256)].rearrange("p (a c) -> p a c", a=4)
                        pool.dma_start(dst, src).then_inc(rpb_landed, 16)
            pool.dma_start(pool_p, inv_cnt).then_inc(inv_landed, 16)
            pool.wait_ge(u_turned, 1)
            pool.dma_start(p2[:, 0, SV:SV + COLS], w_pool).then_inc(wp_landed, 16)
            inverse_root(13, 48)
            pool.wait_ge(head_done, 24 + NA_HEADS)
            pool.dma_start(dft, cs_dft).then_inc(dft_landed, 16)
            inverse_root(14, 2)

        @block.scalar
        def _(act):

            def split(bar, s):
                act.wait_ge(landed[s % RING], 16 * (bar + s // RING + 2))
                act.wait_ge(chunk_used, 4 * bar + s + 1)
                nc.scalar.activation(w_hi[:, s % RING, :], raw[:, s % RING, :], ACT.Copy).then_inc(hi_ready, 1)

            def turn(first, rounds=range(8), banks=TURN_BANKS):
                for r in rounds:
                    act.wait_ge(turned, first + r + 1)
                    nc.scalar.activation(act_hi[:, 2 * r:2 * r + 2, :], ps[banks[r % len(banks)]][:, :].rearrange("p (k t) -> p k t", k=2),
                                         ACT.Copy).then_inc(turn_hi, 1)

            def turn_modulated(first, scale, shift):
                for r in range(8):
                    act.wait_ge(turned, first + r + 1)
                    if r >= 2:
                        act.wait_ge(turn_lo, first + r - 1)
                    for k in range(2):
                        kt = 2 * r + k
                        ins = nc.scalar.activation(gtmp[:, r % 2, k * S:(k + 1) * S], ps[4 + r % 4][:, k * S:(k + 1) * S],
                                                   ACT.Identity, scale=scale(kt), bias=shift(kt))
                    ins.then_inc(turn_hi, 1)

            act.dma_start(C[:, :], consts[0:P, :]).then_inc(consts_landed, 16)
            act.dma_start(V[:, :], vecs).then_inc(consts_landed, 16)
            act.dma_start(onehot, consts[P:P + N_BUCKETS, 0:384]).then_inc(consts_landed, 16)
            act.dma_start(mask_r, consts[P + N_BUCKETS:P + N_BUCKETS + 12, 0:384]).then_inc(consts_landed, 16)
            act.dma_start(lam_in, bass.AP(lam_rows.tensor, 0, [[0, P], [1, DEPTH * 256]])).then_inc(consts_landed, 16)
            act.wait_ge(consts_landed, 80)
            act.wait_ge(rvec_ready, 1)
            act.dma_start(scratch, rvec).then_inc(rvec_stored, 16)
            turn(TURN_X0)
            for r in range(6):
                act.wait_ge(rows_flipped, r + 1)
                ins = nc.scalar.activation(bias_t[:, r * 512:(r + 1) * 512], ps[r % 4][:, :], ACT.Copy)
                ins.then_inc(bias_ready, 1)
            for j in range(RING):
                act.wait_ge(landed[j], 16)
                nc.scalar.activation(w_hi[:, j, :], raw[:, j, :], ACT.Copy).then_inc(hi_ready, 1)
            nc.scalar.activation(csf[:, :], vec["c_cols"], ACT.Silu).then_inc(csf_ready, 1)
            act.wait_ge(lam_dots, 1)
            nc.scalar.activation(lam[:, 4:8], lam[:, 0:4], ACT.Exp).then_inc(lam_exp, 1)

            def copy_group(bank, dst, count=evac_a):
                nc.scalar.activation(dst, ps[bank][:, :], ACT.Copy).then_inc(count, 1)

            def stage_heads(H, q_at, k_at):
                nc.scalar.activation(stage[:, 0:2, :], p1[:, :, bass.ds(q_at, HD)], ACT.Copy)
                nc.scalar.activation(stage[:, 2:4, :], p1[:, :, bass.ds(k_at, HD)], ACT.Copy).then_inc(qk_staged, 1)

            def copy_qkt(H):
                act.wait_ge(qkt_ready, H + 1)
                nc.scalar.activation(qkt[:, 0:512], ps[4][:, :], ACT.Copy).then_inc(qkt_copied, 1)

            def exps(H, parts):
                act.wait_ge(max_ready, H + 1)
                for i, (a, b) in enumerate(parts):
                    ins = nc.scalar.activation(probs[:, a:b], probs[:, a:b], ACT.Exp, bias=nm[:, i:i + 1],
                                               accum_out=sums[:, i:i + 1])
                ins.then_inc(exps_ready, 1)

            def copy_pt(H):
                act.wait_ge(pt_ready, H + 1)
                nc.scalar.activation(p_t, ps[6][:, 0:384], ACT.Copy).then_inc(pt_copied, 1)

            def copy_mod_row():
                nc.scalar.activation(mod_row, ps[2][0:4, :], ACT.Copy).then_inc(mod_row_ready, 1)

            with act.Fori(0, DEPTH) as L:
                B0 = L * LAYER_BARS
                with act.Fori(0, 2) as i:
                    for p in range(2):
                        for s in range(8):
                            split(B0 + 4 * i + 2 * p, s)
                        copy_group(2 * p, p1[:, 0, bass.ds((2 * i + p) * COLS, COLS)])
                for s in range(8):
                    split(B0 + AT_GLU, s)
                    if s == 0:
                        act.wait_ge(evac_a, L * GROUPS_1 + 6)
                        act.wait_ge(evac_d, L * GROUPS_1 + 6)
                        nc.scalar.activation(p1[:, :, CGLU:CGLU + D_C], p1[:, :, CGLU:CGLU + D_C], ACT.Sigmoid)\
                            .then_inc(glu_sig, 1)
                    if s == 1:
                        act.wait_ge(cu_turned, L + 1)
                        for k in range(2):
                            ins = nc.scalar.activation(conv_pad[:, 2 * k:2 * k + 2, CONV - 1:CONV - 1 + S],
                                                       ps[4 + k][:, :].rearrange("p (j t) -> p j t", j=2), ACT.Copy)
                        ins.then_inc(conv_in, 1)
                copy_group(0, p1[:, 0, BV:BV + COLS])
                with act.Fori(0, 2) as hh:
                    with act.Fori(0, 4) as h4:
                        h = 4 * hh + h4
                        H = L * 12 + h
                        for s in range(16):
                            if s == 15:
                                act.wait_ge(chunk_used, 4 * (B0 + AT_L2 + 4 * h) + 16)
                                copy_group(0, p1[:, 0, bass.ds(BV + COLS + h * COLS, COLS)])
                            split(B0 + AT_L2 + 4 * h, s)
                            if s == 0:
                                act.wait_ge(evac_a, L * GROUPS_1 + 7 + 3 * hh)
                                act.wait_ge(evac_d, L * GROUPS_1 + 7 + 3 * hh)
                                stage_heads(H, BQ + hh * B_HALF + h4 * HD, BK + hh * B_HALF + h4 * HD)
                            if s == 2:
                                copy_qkt(H)
                            if s == 4:
                                exps(H, [(0, 128), (128, 384)])
                            if s == 8:
                                copy_pt(H)
                            if s == 14:
                                copy_mod_row()
                act.wait_ge(evac_a, L * GROUPS_1 + 15)
                act.wait_ge(evac_d, L * GROUPS_1 + 15)
                with act.Fori(0, 2) as i:
                    for s in range(24):
                        hh, r = s // 12, s % 12
                        H = L * 12 + B_HEADS + 2 * i + hh
                        if s == 23:
                            act.wait_ge(chunk_used, 4 * (B0 + AT_L3 + 6 * i) + 24)
                            copy_group(0, p1[:, 0, bass.ds(GATE_A + i * COLS, COLS)])
                        if r == 0:
                            at = (2 * i + hh) * HD
                            stage_heads(H, AQ + at, AK + at)
                        split(B0 + AT_L3 + 6 * i, s)
                        if r == 1:
                            copy_qkt(H)
                        if s == 7:
                            g = p1[:, :, bass.ds(GATE_B + i * COLS, COLS)]
                            nc.scalar.activation(g, g, ACT.Silu).then_inc(b_gates_ready, 1)
                        if r == 4:
                            exps(H, [(0, 128), (128, 384), (384, 512), (512, 768)])
                        if r == 9:
                            copy_pt(H)
                        if r == 11:
                            act.wait_ge(pv_ready, H + 1)
                            for t in range(TT):
                                ins = nc.scalar.activation(junk[:, t, :], ps[7][:, t * HD:(t + 1) * HD], ACT.Square,
                                                           accum_out=ss[:, t:t + 1])
                            ins.then_inc(squares_ready, 1)
                        if r == 10:
                            copy_mod_row()
                act.wait_ge(evac_a, L * GROUPS_1 + 17)
                act.wait_ge(evac_d, L * GROUPS_1 + 17)
                nc.scalar.activation(p1[:, :, GATE_A:W1], p1[:, :, GATE_A:W1], ACT.Silu).then_inc(gates_ready, 1)
                turn(8 + 16 * L, range(0, 4), banks=Y_BANKS)
                act.wait_ge(cn_turned, L + 1)
                for j in range(4):
                    ins = nc.scalar.activation(conv_acc[:, j, :], ps[6 + j // 2][:, (j % 2) * S:(j % 2 + 1) * S], ACT.Silu,
                                               scale=vec["conv_g"][:, bass.ds(L * 4 + j, 1)],
                                               bias=vec["conv_beta"][:, bass.ds(L * 4 + j, 1)])
                ins.then_inc(conv_act, 1)
                turn(8 + 16 * L, range(4, 8), banks=Y_BANKS)
                act.dma_start(ctx_tok, ctx_in.rearrange("(t p) d -> p t d", p=P)).then_inc(ctx_landed, 16)
                with act.Fori(0, 2) as i:
                    for p in range(2):
                        for s in range(8):
                            split(B0 + AT_OUT + 4 * i + 2 * p, s)
                turn(16 + 16 * L)

            act.wait_ge(scale_ready, 1)
            turn_modulated(TURN_KVC, lambda k: hs1[:, k, 1:2], lambda k: mod3[:, k, 1:2])
            with act.Fori(0, 2) as i:
                for p in range(2):
                    for s in range(8):
                        split(AT_KVC + 4 * i + 2 * p, s)
                    copy_group(2 * p, kvc[:, 0, bass.ds((2 * i + p) * COLS, COLS)])
            turn_modulated(TURN_H, lambda k: hs1[:, k, 0:1], lambda k: mod3[:, k, 0:1])
            with act.Fori(0, 5) as i:
                for p in range(2):
                    for s in range(8):
                        split(AT_IN2 + 4 * i + 2 * p, s)
                    copy_group(2 * p, p2[:, 0, bass.ds((2 * i + p) * COLS, COLS)])
            heads = [(8 * i + h, rows[:, at + h * HD:at + (h + 1) * HD]) for i, (rows, at) in enumerate(
                [(p2[:, t], at) for at in (NQ, NK) for t in range(TT)] + [(kvc[:, t], 0) for t in range(TT)])
                     for h in range(NA_HEADS)]
            for s in range(8):
                if s == 7:
                    act.wait_ge(chunk_used, 4 * AT_IN2 + 88)
                    copy_group(0, p2[:, 0, FT:FT + COLS])
                split(AT_IN2 + 20, s)
                if s == 1:
                    act.wait_ge(pool_turned, 1)
                    act.wait_ge(cleared, 4)
                    for k in range(2):
                        ins = nc.scalar.activation(pool_u[:, 2 * k:2 * k + 2, 8:8 + S],
                                                   ps[2 + k][:, :].rearrange("p (j t) -> p j t", j=2), ACT.Copy)
                    ins.then_inc(pool_copied, 1)
                if s == 2:
                    act.wait_ge(u_turned, 1)
                    for k in range(2):
                        ins = nc.scalar.activation(conv_pad[:, 2 * k:2 * k + 2, CONV - 1:CONV - 1 + S],
                                                   ps[4 + k][:, :].rearrange("p (j t) -> p j t", j=2), ACT.Copy)
                    ins.then_inc(u_copied, 1)
                if s == 0:
                    act.wait_ge(evac_a, 46)
                    act.wait_ge(evac_d, 46)
                else:
                    act.wait_ge(squares_ready, DEPTH * A_HEADS + s)
                for n, (col, rows) in enumerate(heads[6 * s:6 * s + 6]):
                    ins = nc.scalar.activation(gflat[:, n * HD:(n + 1) * HD], rows, ACT.Square, accum_out=ss[:, col:col + 1])
                ins.then_inc(squares_ready, 1)
            act.wait_ge(pool_out, 1)
            act.wait_ge(u_used, 1)
            for g in range(4):
                ins = nc.scalar.activation(pool_v[:, g, :], ps[4 + g // 2][:, (g % 2) * S:(g % 2 + 1) * S], ACT.Copy,
                                           scale=vec["pool_scale"][:, g:g + 1])
            ins.then_inc(pool_scaled, 1)

            def na_stage(h):
                for i, src in enumerate([p2[:, 0], p2[:, 1]]):
                    nc.scalar.activation(stage[:, i, :], src[:, bass.ds(NQ + h * HD, HD)], ACT.Copy,
                                         scale=rstd[:, bass.ds(8 * i + h, 1)])
                    nc.scalar.activation(stage[:, 2 + i, :], src[:, bass.ds(NK + h * HD, HD)], ACT.Copy,
                                         scale=rstd[:, bass.ds(8 * (2 + i) + h, 1)])
                    ins = nc.scalar.activation(stage[:, 4 + i, :], kvc[:, i, bass.ds(h * HD, HD)], ACT.Copy,
                                               scale=rstd[:, bass.ds(8 * (4 + i) + h, 1)])
                ins.then_inc(qk_staged, 1)

            for turn_of, branch in enumerate((3, 2, 1)):
                with act.Fori(0, 2) as i:
                    for s in range(20):
                        n, r = 2 * i + s // 10, s % 10
                        g = 4 * turn_of + n
                        H = 24 + g
                        split(AT_GATES + 10 * turn_of + 5 * i, s)
                        if r == 7:
                            act.wait_ge(gate_added, g + 1)
                            nc.scalar.activation(gtmp[:, 0, :], ps[0][:, :], ACT.Sigmoid)
                            nc.scalar.activation(gtmp[:, 1, :], ps[1][:, :], ACT.Sigmoid).then_inc(sig_done, 1)
                        if turn_of == 2:
                            continue
                        if r == 0:
                            act.wait_ge(pv_ready, H)
                            act.wait_ge(rstd_ready, 14)
                            na_stage(g)
                        if r == 2:
                            act.wait_ge(qkt_ready, H + 1)
                            nc.scalar.activation(qkt[:, 0:256], ps[4][:, 0:256], ACT.Copy, scale=vec["q_norm"][:, 0:1])
                            nc.scalar.activation(qkt[:, 256:512], ps[4][:, 256:512], ACT.Copy, scale=vec["k_norm"][:, 0:1])
                            nc.scalar.activation(qkt[:, 512:768], ps[5][:, 0:256], ACT.Copy, scale=vec["k_norm"][:, 0:1])\
                                .then_inc(qkt_copied, 1)
                        if r == 4:
                            exps(H, [(0, 512), (512, 1024)])
                        if r == 6:
                            act.wait_ge(pt_ready, H + 1)
                            nc.scalar.activation(na_pt[:, 0:512], ps[4][:, :], ACT.Copy)
                            nc.scalar.activation(na_pt[:, 512:1024], ps[5][:, :], ACT.Copy).then_inc(pt_copied, 1)
                if turn_of == 1:
                    for r in range(8):
                        act.wait_ge(row_ready, r + 1)
                        at = (NV, NK)[r // 4] + (r % 2) * COLS
                        nc.scalar.activation(p2[:, (r % 4) // 2, at:at + COLS], ps[6 + r % 2][:, :], ACT.Copy)\
                            .then_inc(row_copied, 1)
                    for g in range(4):
                        act.wait_ge(ft_cols, g + 1)
                        nc.scalar.activation(ft_by_pos[:, g, :], ps[4 + g][:, :], ACT.Copy).then_inc(ft_copied, 1)
            with act.Fori(0, 2) as i:
                for p in range(2):
                    for s in range(8):
                        split(AT_GATE0 + 4 * i + 2 * p, s)
                    for t in range(TT):
                        ins = nc.scalar.activation(kvc[:, t, bass.ds((2 * i + p) * COLS, COLS)], ps[2 * p + t][:, :], ACT.Sigmoid)
                    ins.then_inc(sig_done, 1)
            turn(TURN_NA, range(4))
            with act.Fori(0, 2) as i:
                for s in range(8):
                    split(AT_NAP + 2 * i, s)
            turn(TURN_Y2)
            with act.Fori(0, 2) as i:
                for p in range(2):
                    for s in range(8):
                        split(AT_WO + 4 * i + 2 * p, s)
            act.wait_ge(scale_ready, 2)
            turn_modulated(TURN_H2, lambda k: hs2[:, k:k + 1], lambda k: mod3[:, 3 * KT + k, 0:1])

            def silus():
                for t in range(TT):
                    ins = nc.scalar.activation(gtmp[:, t, :], ps[t][:, :], ACT.Silu)
                ins.then_inc(silu_done, 1)

            def hidden_hi(f):
                act.wait_ge(hid_turned, f + 1)
                for k in range(2):
                    ins = nc.scalar.activation(br_hi[:, 2 * k:2 * k + 2, :], ps[4 + k][:, :].rearrange("p (j t) -> p j t", j=2), ACT.Copy)
                ins.then_inc(hid_hi, 1)

            for s in range(16):
                split(AT_FF, s)
                if s == 7:
                    act.wait_ge(turn_lo, TURN_H2 + 8)
                    silus()
            with act.Fori(0, FF - 1) as i:
                for s in range(24):
                    split(AT_FF + 4 + 6 * i, s)
                    if s == 7:
                        act.wait_ge(hid_ready, i + 1)
                        silus()
                        hidden_hi(i)
            hidden_hi(FF - 1)
            for s in range(4):
                split(BARS - 2, s)

        @block.tensor
        def _(pe):
            def chunk(bar, s, tiles):
                pe.wait_ge(lo_ready, 4 * bar + s + 1)
                for u, (hi, lo, kt, banks, first, last) in enumerate(tiles):
                    wh = w_hi[:, s % RING, u * COLS:(u + 1) * COLS]
                    wl = w_lo[:, s % RING, u * COLS:(u + 1) * COLS]
                    for t in range(TT):
                        xh, xl = hi[:, kt, t * P:(t + 1) * P], lo[:, kt, t * P:(t + 1) * P]
                        acc = ps[banks[t]][:, :]
                        nc.tensor.matmul(acc, xh, wh, start=first, stop=False)
                        nc.tensor.matmul(acc, xh, wl, start=False, stop=False)
                        mm = nc.tensor.matmul(acc, xl, wh, start=False, stop=last)
                mm.then_inc(chunk_used, 1)

            def of_group(s, banks, tiles=KT, hi=None, lo=None):
                hi, lo = (act_hi, act_lo) if hi is None else (hi, lo)
                return [(hi, lo, 2 * s + u, banks, 2 * s + u == 0, 2 * s + u == tiles - 1) for u in range(2)]

            def mod_chunk(bar, s, k):
                pe.wait_ge(lo_ready, 4 * bar + s + 1)
                for u in range(2):
                    kt = 2 * k + u
                    for w in (w_hi, w_lo):
                        mm = nc.tensor.matmul(ps[2][:, :], cs_flat[:, 4 * kt:4 * kt + P], w[:, s % RING, u * COLS:(u + 1) * COLS],
                                              start=kt == 0 and w is w_hi, stop=kt == KT - 1 and w is w_lo)
                mm.then_inc(chunk_used, 1)

            def mod_columns(M):
                pe.wait_ge(mod_row_ready, M + 1)
                for j in range(4):
                    mm = nc.tensor.matmul(ps[3][:, 2 * j:2 * j + 2], mod_row[:, j * P:(j + 1) * P], comb, start=True, stop=True)
                mm.then_inc(mod_col_ready, 1)

            def turn(first, src, rounds=range(8), ready=None, banks=TURN_BANKS):
                for r in rounds:
                    if ready is not None:
                        ready(r)
                    if r >= len(banks):
                        pe.wait_ge(turn_lo, first + r - len(banks) + 1)
                    for k in range(2):
                        for t in range(TT):
                            at = k * S + t * P
                            mm = nc.tensor.transpose(ps[banks[r % len(banks)]][:, at:at + P], src(t, 2 * r + k), ident)
                    mm.then_inc(turned, 1)

            def turn_cols(banks, src, count=None):
                for j in range(4):
                    for t in range(TT):
                        at = (j % 2) * S + t * P
                        mm = nc.tensor.transpose(ps[banks[j // 2]][:, at:at + P], src(t, j), ident)
                if count is not None:
                    mm.then_inc(count, 1)

            pe.wait_ge(consts_landed, 80)
            nc.tensor.matmul(ps[0][0:12, 0:384], vec["rel_bias"][0:N_BUCKETS, :], onehot, start=True, stop=True).then_inc(rel_ready, 1)
            pe.wait_ge(x_landed, 16)
            turn(TURN_X0, lambda t, k: x[:, t, k * P:(k + 1) * P])
            pe.wait_ge(rows_landed, 16)
            for r in range(6):
                if r >= 4:
                    pe.wait_ge(bias_ready, r - 3)
                nc.tensor.matmul(ps[r % 4][:, :], flip, flat[:, r * 512:(r + 1) * 512], start=True, stop=True).then_inc(rows_flipped, 1)
            pe.wait_ge(bias_ready, 6)

            def turn_heads(H, n=4):
                pe.wait_ge(qk_staged, H + 1)
                for i in range(n):
                    mm = nc.tensor.transpose(ps[4 + i // 4][:, (i % 4) * P:(i % 4 + 1) * P], stage[:, i, :], ident)
                mm.then_inc(qkt_ready, 1)

            def scores(bank, rows):
                q, k = qkt[rows, 0:256], qkt[rows, 256:512]
                nc.tensor.matmul(ps[bank][:, 0:128], q[:, 0:128], k[:, 0:128], start=True, stop=True)
                return nc.tensor.matmul(ps[bank][:, 128:384], q[:, 128:256], k, start=True, stop=True)

            def turn_probs():
                for i in range(3):
                    mm = nc.tensor.transpose(ps[6][:, i * P:(i + 1) * P], probs[:, i * P:(i + 1) * P], ident)
                mm.then_inc(pt_ready, 1)

            def weigh_values(H, at):
                pe.wait_ge(pt_copied, H + 1)
                v = [p1[:, t, bass.ds(at, HD)] for t in range(TT)]
                nc.tensor.matmul(ps[7][:, 0:HD], p_t[:, 0:128], v[0], start=True, stop=True)
                nc.tensor.matmul(ps[7][:, HD:2 * HD], p_t[:, 128:256], v[0], start=True, stop=False)
                nc.tensor.matmul(ps[7][:, HD:2 * HD], p_t[:, 256:384], v[1], start=False, stop=True).then_inc(pv_ready, 1)

            with pe.Fori(0, DEPTH) as L:
                B0 = L * LAYER_BARS
                with pe.Fori(0, 2) as i:
                    for p in range(2):
                        for e in (evac_a, evac_d):
                            pe.wait_ge(e, L * GROUPS_1 + 2 * i + p + 1)
                        for s in range(8):
                            if p == 0:
                                pe.wait_ge(turn_lo, 16 * L + s + 1)
                            chunk(B0 + 4 * i + 2 * p, s, of_group(s, (2 * p, 2 * p + 1)))
                for e in (evac_a, evac_d):
                    pe.wait_ge(e, L * GROUPS_1 + 3 + 2)
                for s in range(8):
                    chunk(B0 + AT_GLU, s, of_group(s, (0, 1)))
                    if s == 1:
                        pe.wait_ge(glu_ready, L + 1)
                        turn_cols((4, 5), lambda t, j: p1[:, t, CU + j * P:CU + (j + 1) * P], cu_turned)
                with pe.Fori(0, 2) as hh:
                    with pe.Fori(0, 4) as h4:
                        h = 4 * hh + h4
                        H, bar = L * 12 + h, B0 + AT_L2 + 4 * h
                        pe.wait_ge(cs_ready, 1)
                        for e in (evac_a, evac_d):
                            pe.wait_ge(e, L * GROUPS_1 + 4 + 2)
                        for s in range(16):
                            if s == 2:
                                for e in (evac_a, evac_d):
                                    pe.wait_ge(e, L * GROUPS_1 + 5 + 2 + h)
                            part, k = MIX[s]
                            if part == "group":
                                chunk(bar, s, of_group(k, (0, 1)))
                            else:
                                mod_chunk(bar, s, k)
                            if s == 2:
                                turn_heads(H)
                            if s == 4:
                                pe.wait_ge(qkt_copied, H + 1)
                                scores(5, slice(0, P)).then_inc(scores_ready, 1)
                            if s == 8:
                                pe.wait_ge(exps_ready, H + 1)
                                turn_probs()
                            if s == 11:
                                weigh_values(H, BV + hh * B_HALF + h4 * HD)
                        mod_columns(L * 12 + h)
                with pe.Fori(0, 2) as i:
                    for s in range(24):
                        hh, r = s // 12, s % 12
                        h = 2 * i + hh
                        H, bar = L * 12 + B_HEADS + h, B0 + AT_L3 + 6 * i
                        if s == 2:
                            for e in (evac_a, evac_d):
                                pe.wait_ge(e, L * GROUPS_1 + 13 + 2 + i)
                        if r % 3 == 2:
                            chunk(bar, s, of_group(4 * hh + r // 3, (0, 1)))
                        else:
                            mod_chunk(bar, s, 2 * (r // 3) + r % 3)
                        if r == 1:
                            turn_heads(H)
                        if r == 3:
                            pe.wait_ge(qkt_copied, H + 1)
                            scores(5, slice(0, 64))
                            scores(6, slice(64, 128)).then_inc(scores_ready, 1)
                        if r == 9:
                            pe.wait_ge(diff_ready, L * A_HEADS + h + 1)
                            turn_probs()
                        if r == 10:
                            weigh_values(H, AV + h * HD)
                        if r == 11:
                            mod_columns(H)
                pe.wait_ge(conv_tapped, CONV * (L + 1))
                for t in range(TT):
                    for j in range(4):
                        mm = nc.tensor.transpose(ps[4 + t][:, j * P:(j + 1) * P], conv_acc[:, j, t * P:(t + 1) * P], ident)
                mm.then_inc(conv_turned, 1)
                y_cols = lambda t, k: p1[:, t, GATE + k * P:GATE + (k + 1) * P]
                pe.wait_ge(b_gated, 2 * (L + 1))
                turn(8 + 16 * L, y_cols, range(0, 1), banks=Y_BANKS)
                for e in (evac_a, evac_d):
                    pe.wait_ge(e, L * GROUPS_1 + GROUPS_1 + 2)
                turn(8 + 16 * L, y_cols, range(1, 3), banks=Y_BANKS)
                pe.wait_ge(mod_done, 12 * (L + 1))
                turn(8 + 16 * L, y_cols, range(3, 4), banks=Y_BANKS)
                pe.wait_ge(cn_ready, L + 1)
                turn_cols((6, 7), lambda t, j: p1[:, t, AK + j * P:AK + (j + 1) * P], cn_turned)
                pe.wait_ge(a_gated, L + 1)
                pe.wait_ge(turn_lo, 12 + 16 * L)
                turn(8 + 16 * L, y_cols, range(4, 6), banks=Y_BANKS)
                pe.wait_ge(conv_act, L + 1)
                pe.wait_ge(cpw_landed, 64 * (L + 1))
                pe.wait_ge(conv_act, 1)
                for t in range(TT):
                    for j in range(4):
                        at = CU + (j % 2) * COLS
                        mm = nc.tensor.matmul(ps[t][:, :], conv_acc[:, j, t * P:(t + 1) * P], p1[:, j // 2, at:at + COLS],
                                              start=j == 0, stop=j == 3)
                mm.then_inc(cpw_ready, 1)
                pe.wait_ge(y_ready, L + 1)
                turn(8 + 16 * L, y_cols, range(6, 8), banks=Y_BANKS)
                with pe.Fori(0, 2) as i:
                    for p in range(2):
                        pe.wait_ge(x_summed, L * 4 + 2 * i + p + 1)
                        for s in range(8):
                            if p == 0:
                                pe.wait_ge(turn_lo, 8 + 16 * L + s + 1)
                            chunk(B0 + AT_OUT + 4 * i + 2 * p, s, of_group(s, (2 * p, 2 * p + 1)))
                turn(16 + 16 * L, lambda t, k: x[:, t, k * P:(k + 1) * P],
                     ready=lambda r: pe.wait_ge(x_ready, 4 * L + r // 2 + 1))

            pe.wait_ge(ctx_ready, 2)
            pe.wait_ge(turn_lo, TURN_KVC)
            turn(TURN_KVC, lambda t, k: ctx_tok[:, t, k * P:(k + 1) * P])
            with pe.Fori(0, 2) as i:
                for p in range(2):
                    for e in (evac_a, evac_d):
                        pe.wait_ge(e, 30 + 2 * i + p + 1)
                    for s in range(8):
                        if p == 0:
                            pe.wait_ge(turn_lo, TURN_KVC + s + 1)
                        chunk(AT_KVC + 4 * i + 2 * p, s, of_group(s, (2 * p, 2 * p + 1)))
                pe.wait_ge(rpb_landed, 256 * (i + 1))
                for n in range(4):
                    nc.tensor.matmul(ps[4 + n][:, :], flip, rpb_rows[:, n * 512:(n + 1) * 512], start=True, stop=True)\
                        .then_inc(na_flipped, 1)
            pe.wait_ge(xn_ready, 1)
            pe.wait_ge(na_biased, 8)
            turn(TURN_H, lambda t, k: xn[:, t, k * P:(k + 1) * P])
            with pe.Fori(0, 5) as i:
                for p in range(2):
                    for e in (evac_a, evac_d):
                        pe.wait_ge(e, 34 + 2 * i + p + 1)
                    for s in range(8):
                        if p == 0:
                            pe.wait_ge(turn_lo, TURN_H + s + 1)
                        chunk(AT_IN2 + 4 * i + 2 * p, s, of_group(s, (2 * p, 2 * p + 1)))
            for e in (evac_a, evac_d):
                pe.wait_ge(e, 44 + 1)
            for s in range(8):
                chunk(AT_IN2 + 20, s, of_group(s, (0, 1)))
                if s == 1:
                    for e in (evac_a, evac_d):
                        pe.wait_ge(e, 44 + 2)
                    turn_cols((2, 3), lambda t, j: p2[:, t, POOL + j * P:POOL + (j + 1) * P], pool_turned)
                if s == 2:
                    pe.wait_ge(u_ready, 1)
                    turn_cols((6, 7), lambda t, j: p2[:, t, SB + j * P:SB + (j + 1) * P])
                    turn_cols((4, 5), lambda t, j: p2[:, t, SV + j * P:SV + (j + 1) * P], u_turned)
            for e in (evac_a, evac_d):
                pe.wait_ge(e, 45 + 2)
            pe.wait_ge(pool_ready, 1)
            pe.wait_ge(wp_landed, 16)
            pe.wait_ge(u_copied, 1)
            for g in range(4):
                mm = nc.tensor.matmul(ps[4 + g // 2][:, (g % 2) * S:(g % 2 + 1) * S], p2[:, 0, SV + g * P:SV + (g + 1) * P],
                                      pool_p[:, g, :], start=True, stop=True)
            mm.then_inc(pool_out, 1)

            for turn_of in range(3):
                with pe.Fori(0, 2) as i:
                    for s in range(20):
                        n, r = 2 * i + s // 10, s % 10
                        g = 4 * turn_of + n
                        H = 24 + g
                        if r == 0:
                            pe.wait_ge(sig_done, g + 1)
                        if r == 8:
                            pe.wait_ge(br_ready, turn_of + 1)
                            pe.wait_ge(gate_added, g + 1)
                        chunk(AT_GATES + 10 * turn_of + 5 * i, s,
                              of_group(r, (0, 1)) if r < 8 else of_group(r - 8, (2, 3), 4, br_hi, br_lo))
                        if turn_of == 2:
                            continue
                        if r == 2:
                            pe.wait_ge(pool_scaled, 1)
                            turn_heads(H, 6)
                        if r == 4:
                            pe.wait_ge(br_ready, 1)
                            pe.wait_ge(qkt_copied, H + 1)
                            for t in range(TT):
                                mm = nc.tensor.matmul(ps[6 + t][:, :], qkt[:, t * P:(t + 1) * P], qkt[:, 256:768], start=True, stop=True)
                            mm.then_inc(scores_ready, 1)
                        if r == 6:
                            pe.wait_ge(exps_ready, H + 1)
                            for t in range(TT):
                                for k in range(4):
                                    at = (k % 2) * S + t * P
                                    mm = nc.tensor.transpose(ps[4 + k // 2][:, at:at + P],
                                                             probs[:, t * 512 + k * P:t * 512 + (k + 1) * P], ident)
                            mm.then_inc(pt_ready, 1)
                        if r == 8:
                            pe.wait_ge(pt_copied, H + 1)
                            for t in range(TT):
                                for k in range(4):
                                    v = p2[:, k, bass.ds(NV + g * HD, HD)] if k < 2 else kvc[:, k - 2, bass.ds(1024 + g * HD, HD)]
                                    mm = nc.tensor.matmul(ps[6][:, t * HD:(t + 1) * HD], na_pt[:, k * S + t * P:k * S + (t + 1) * P], v,
                                                          start=k == 0, stop=k == 3)
                            mm.then_inc(pv_ready, 1)
                if turn_of == 1:
                    pe.wait_ge(head_done, 24 + NA_HEADS)
                    for r in range(8):
                        if r >= 2:
                            pe.wait_ge(row_copied, r - 1)
                        pe.wait_ge(diag_ready, r + 1)
                        d = early_diag[:, r, :] if r < 2 else diag[:, (r - 2) % 4, :]
                        nc.tensor.matmul(ps[6 + r % 2][:, :], ones[:, :], d, start=True, stop=True).then_inc(row_ready, 1)
                    pe.wait_ge(dft_landed, 16)
                    pe.wait_ge(row_copied, 8)
                    for g in range(4):
                        for t in range(TT):
                            mm = nc.tensor.matmul(ps[4 + g][:, :], p2[:, t, FT + g * P:FT + (g + 1) * P], dft[:, t * 512:(t + 1) * 512],
                                                  start=t == 0, stop=t == TT - 1)
                        mm.then_inc(ft_cols, 1)
                    pe.wait_ge(ft_copied, 4)
                    for g in range(4):
                        o = ps[4 + g // 2][:, (g % 2) * S:(g % 2 + 1) * S]
                        nc.tensor.matmul(o, dft[:, 1024:1152], ft_by_pos[:, g, 0:S], start=True, stop=False)
                        mm = nc.tensor.matmul(o, dft[:, 1152:1280], ft_by_pos[:, g, S:2 * S], start=False, stop=True)
                    mm.then_inc(ft_ready, 1)
            with pe.Fori(0, 2) as i:
                for p in range(2):
                    if p:
                        pe.wait_ge(gate_added, 13)
                    pe.wait_ge(sig_done, 13 + (i if p == 0 else 2 * i))
                    for s in range(8):
                        chunk(AT_GATE0 + 4 * i + 2 * p, s, of_group(s, (2 * p, 2 * p + 1)))
            turn(TURN_NA, lambda t, k: p2[:, t, NQ + k * P:NQ + (k + 1) * P], range(4))
            pe.wait_ge(sig_done, 17)
            with pe.Fori(0, 2) as i:
                for s in range(8):
                    p = s // 4
                    if s % 4 == 0:
                        pe.wait_ge(gate_added, 12 + 2 * i + p)
                    if s < 4:
                        pe.wait_ge(turn_lo, TURN_NA + s + 1)
                    chunk(AT_NAP + 2 * i, s, of_group(s % 4, (2 * p, 2 * p + 1), 8))
            pe.wait_ge(gate_added, 17)
            turn(TURN_Y2, lambda t, k: p2[:, t, Y2 + k * P:Y2 + (k + 1) * P])
            with pe.Fori(0, 2) as i:
                for p in range(2):
                    pe.wait_ge(x_summed, 8 + 2 * i + p + 1)
                    for s in range(8):
                        if p == 0:
                            pe.wait_ge(turn_lo, TURN_Y2 + s + 1)
                        chunk(AT_WO + 4 * i + 2 * p, s, of_group(s, (2 * p, 2 * p + 1)))
            turn(TURN_H2, lambda t, k: kvc[:, t, k * P:(k + 1) * P], ready=lambda r: pe.wait_ge(h2_ready, r // 2 + 1))

            def turn_hidden(f):
                pe.wait_ge(hid_ready, f + 1)
                turn_cols((4, 5), lambda t, j: kvc[:, t, j * P:(j + 1) * P], hid_turned)

            def down(bar, s0, s, f):
                n = s // 2
                if s == 0:
                    pe.wait_ge(hid_lo, f + 1)
                if s % 2 == 0:
                    pe.wait_ge(acc_done, 4 * f + n + 1)
                chunk(bar, s0 + s, of_group(s % 2, (4, 5) if n % 2 else (6, 7), 4, br_hi, br_lo))

            for s in range(16):
                if s < 8:
                    pe.wait_ge(turn_lo, TURN_H2 + s + 1)
                chunk(AT_FF, s, of_group(s % 8, (0, 1) if s < 8 else (2, 3)))
            with pe.Fori(0, FF - 1) as i:
                bar = AT_FF + 4 + 6 * i
                for s in range(24):
                    if s == 0:
                        pe.wait_ge(silu_done, i + 1)
                    if s == 8:
                        pe.wait_ge(hid_ready, i + 1)
                    if s < 16:
                        chunk(bar, s, of_group(s % 8, (0, 1) if s < 8 else (2, 3)))
                    else:
                        down(bar, 16, s - 16, i)
                    if s == 7:
                        pe.wait_ge(acc_done, 4 * i + 2)
                        turn_hidden(i)
            pe.wait_ge(acc_done, 4 * (FF - 1) + 2)
            turn_hidden(FF - 1)
            for s in range(8):
                down(BARS - 2, 0, s, FF - 1)

        @block.vector
        def _(dve):
            ch = Chain(dve, dve_chain)

            def split(bar, s):
                dve.wait_ge(hi_ready, 4 * bar + s + 5)
                j = s % RING
                nc.vector.tensor_tensor(w_lo[:, j, :], raw[:, j, :], w_hi[:, j, :].bitcast(F32), ALU.subtract).then_inc(lo_ready, 1)

            def rest_of(dst, src, hi):
                return nc.vector.tensor_tensor(dst, src, hi.bitcast(F32), ALU.subtract)

            def turn(first, rounds=range(8), banks=TURN_BANKS):
                for r in rounds:
                    dve.wait_ge(turn_hi, first + r + 1)
                    a = slice(2 * r, 2 * r + 2)
                    rest_of(act_lo[:, a, :], ps[banks[r % len(banks)]][:, :].rearrange("p (k t) -> p k t", k=2), act_hi[:, a, :])\
                        .then_inc(turn_lo, 1)

            def turn_modulated(first):
                for r in range(8):
                    dve.wait_ge(turn_hi, first + r + 1)
                    a = slice(2 * r, 2 * r + 2)
                    v = gtmp[:, r % 2, :].rearrange("p (k t) -> p k t", k=2)
                    ch.link(nc.vector.tensor_copy(act_hi[:, a, :], v))
                    rest_of(act_lo[:, a, :], v, act_hi[:, a, :]).then_inc(turn_lo, 1)

            dve.wait_ge(consts_landed, 80)
            pairs = lam_in.rearrange("p (n two d) -> p n two d", two=2, d=64)
            ch.link(nc.vector.tensor_tensor(probs[:, 0:256].rearrange("p (b d) -> p b d", d=64), pairs[:, :, 0, :], pairs[:, :, 1, :], ALU.mult))
            nc.vector.reduce_sum(lam[:, 0:4], probs[:, 0:256].rearrange("p (b d) -> p b d", d=64), AX_X).then_inc(lam_dots, 1)
            for layer in range(DEPTH):
                g = vec["head_gain"][:, layer * HD:(layer + 1) * HD]
                ch.link(nc.vector.tensor_scalar(g, g, 1.0 - LAM_INIT[layer], None, ALU.mult))
            dve.wait_ge(rel_ready, 1)
            nc.vector.tensor_tensor(rvec, ps[0][0:12, 0:384], mask_r, ALU.add).then_inc(rvec_ready, 1)
            turn(TURN_X0)
            for j in range(RING):
                dve.wait_ge(hi_ready, j + 1)
                nc.vector.tensor_tensor(w_lo[:, j, :], raw[:, j, :], w_hi[:, j, :].bitcast(F32), ALU.subtract).then_inc(lo_ready, 1)
            dve.wait_ge(csf_ready, 1)
            c2 = csf[:, :].rearrange("p (k c) -> p k c", c=2)
            ch.link(nc.vector.tensor_copy(cs[:, :, 0:2], c2))
            nc.vector.memset(cs_flat[:, 4 * KT:4 * KT + P - 4].bitcast(F32), 0.0)
            rest_of(cs[:, :, 2:4], c2, cs[:, :, 0:2]).then_inc(cs_ready, 1)
            dve.wait_ge(lam_exp, 1)
            e = lam[:, 4:8].rearrange("p (l two) -> p l two", two=2)
            ch.link(nc.vector.tensor_tensor(small[:, 56:58].rearrange("p (l o) -> p l o", o=1), e[:, :, 1:2], e[:, :, 0:1], ALU.subtract))
            for layer in range(DEPTH):
                ch.link(nc.vector.tensor_scalar(lam[:, layer:layer + 1], small[:, 56 + layer:57 + layer], LAM_INIT[layer], None, ALU.subtract))
            dve.wait_ge(bias_ready, 6)

            def copy_group(bank, dst):
                nc.vector.tensor_copy(dst, ps[bank][:, :]).then_inc(evac_d, 1)

            def biased_scores(bank, at, head_bias, scale):
                nc.vector.scalar_tensor_tensor(probs[:, at:at + 128], ps[bank][:, 0:128], scale, bias_t[:, bass.ds(head_bias + 128, 128)], ALU.mult, ALU.add)
                ch.link(nc.vector.scalar_tensor_tensor(probs[:, at + 128:at + 384], ps[bank][:, 128:384], scale, bias_t[:, bass.ds(head_bias, 256)],
                                                       ALU.mult, ALU.add))

            def row_maxima(parts):
                for i, (a, b) in enumerate(parts):
                    ins = nc.vector.reduce_max(mx[:, i:i + 1], probs[:, a:b], AX_X)
                ch.link(ins)
                n = len(parts)
                nc.vector.tensor_scalar(nm[:, 0:n], mx[:, 0:n], -1.0, None, ALU.mult).then_inc(max_ready, 1)

            def add_mod(M):
                dve.wait_ge(mod_col_ready, M + 1)
                nc.vector.tensor_tensor(mod_t[:, bass.ds(M * 8, 8)], ps[3][:, 0:8], vec["b_mod"][:, bass.ds(M * 8, 8)], ALU.add).then_inc(mod_done, 1)

            def tap(L, k, before):
                dve.wait_ge(conv_tapped, L * CONV + before)
                for j in range(4):
                    ins = nc.vector.scalar_tensor_tensor(conv_acc[:, j, :], conv_pad[:, j, bass.ds(k, S)],
                                                         vec["conv_dw"][:, bass.ds(L * (4 * CONV) + j * CONV + k, 1)], conv_acc[:, j, :],
                                                         ALU.mult, ALU.add)
                ins.then_inc(conv_tapped, 1)

            with dve.Fori(0, DEPTH) as L, ch.loop(L, DEPTH, DVE_LAYER):
                B0 = L * LAYER_BARS
                with dve.Fori(0, 2) as i:
                    for p in range(2):
                        for s in range(8):
                            split(B0 + 4 * i + 2 * p, s)
                        dve.wait_ge(chunk_used, 4 * B0 + 16 * i + 8 * p + 8)
                        copy_group(2 * p + 1, p1[:, 1, bass.ds((2 * i + p) * COLS, COLS)])
                for s in range(8):
                    split(B0 + AT_GLU, s)
                    if s == 0:
                        dve.wait_ge(glu_sig, L + 1)
                        nc.vector.tensor_tensor(p1[:, :, CU:CU + D_C], p1[:, :, CU:CU + D_C], p1[:, :, CGLU:CGLU + D_C], ALU.mult)\
                            .then_inc(glu_ready, 1)
                    if s == 2:
                        dve.wait_ge(conv_in, L + 1)
                        k = CONV - 1
                        for j in range(4):
                            ins = nc.vector.tensor_scalar(conv_acc[:, j, :], conv_pad[:, j, k:k + S],
                                                          vec["conv_dw"][:, bass.ds(L * (4 * CONV) + j * CONV + k, 1)],
                                                          vec["conv_b"][:, bass.ds(L * 4 + j, 1)], ALU.mult, ALU.add)
                        ins.then_inc(conv_tapped, 1)
                    if s in (3, 4):
                        tap(L, CONV + 1 - s, s - 2)
                dve.wait_ge(chunk_used, 4 * B0 + 4 * AT_GLU + 8)
                copy_group(1, p1[:, 1, BV:BV + COLS])
                with dve.Fori(0, 2) as hh, ch.loop(hh, 2, 4 * DVE_B):
                    with dve.Fori(0, 4) as h4, ch.loop(h4, 4, DVE_B):
                        h = 4 * hh + h4
                        H = L * 12 + h
                        for s in range(16):
                            if s == 15:
                                dve.wait_ge(chunk_used, 4 * B0 + 4 * AT_L2 + 16 * h + 16)
                                copy_group(1, p1[:, 1, bass.ds(BV + COLS + h * COLS, COLS)])
                            split(B0 + AT_L2 + 4 * h, s)
                            if s in (1, 7, 13):
                                tap(L, 3 * h + s // 6, 3 * h + s // 6 + 3)
                            if s == 4:
                                dve.wait_ge(scores_ready, H + 1)
                                biased_scores(5, 0, (A_HEADS + h) * S, HEAD_SCALE)
                                row_maxima([(0, 128), (128, 384)])
                            if s == 8:
                                dve.wait_ge(exps_ready, H + 1)
                                ch.link(nc.vector.reciprocal(recip[:, 0:2], sums[:, 0:2]))
                            if s == 11:
                                dve.wait_ge(pv_ready, H + 1)
                                for t in range(TT):
                                    ins = nc.vector.tensor_scalar(p1[:, t, bass.ds(BQ + hh * B_HALF + h4 * HD, HD)], ps[7][:, t * HD:(t + 1) * HD],
                                                                  recip[:, t:t + 1], None, ALU.mult)
                                ins.then_inc(head_done, 1)
                        add_mod(L * 12 + h)
                with dve.Fori(0, 2) as i, ch.loop(i, 2, DVE_A):
                    for s in range(24):
                        hh, r = s // 12, s % 12
                        h = 2 * i + hh
                        H = L * 12 + B_HEADS + h
                        if s == 23:
                            dve.wait_ge(chunk_used, 4 * B0 + 4 * AT_L3 + 24 * i + 24)
                            copy_group(1, p1[:, 1, bass.ds(GATE_A + i * COLS, COLS)])
                        split(B0 + AT_L3 + 6 * i, s)
                        if r == 1:
                            tap(L, 24 + h, 27 + h)
                        if r == 3:
                            dve.wait_ge(scores_ready, H + 1)
                            biased_scores(5, 0, h * S, A_SCALE)
                            biased_scores(6, 384, h * S, A_SCALE)
                            row_maxima([(0, 128), (128, 384), (384, 512), (512, 768)])
                        if r == 5:
                            dve.wait_ge(exps_ready, H + 1)
                            ch.link(nc.vector.reciprocal(recip[:, 0:4], sums[:, 0:4]))
                            ch.link(nc.vector.tensor_scalar(nlr[:, 0:2], recip[:, 2:4], lam[:, bass.ds(L, 1)], None, ALU.mult))
                            nc.vector.tensor_scalar(probs[:, 384:512], probs[:, 384:512], nlr[:, 0:1], None, ALU.mult)
                            ch.link(nc.vector.tensor_scalar(probs[:, 512:768], probs[:, 512:768], nlr[:, 1:2], None, ALU.mult))
                            nc.vector.scalar_tensor_tensor(probs[:, 0:128], probs[:, 0:128], recip[:, 0:1], probs[:, 384:512], ALU.mult, ALU.add)
                            nc.vector.scalar_tensor_tensor(probs[:, 128:384], probs[:, 128:384], recip[:, 1:2], probs[:, 512:768], ALU.mult, ALU.add)\
                                .then_inc(diff_ready, 1)
                        if s == 13:
                            dve.wait_ge(head_done, L * 12 + B_HEADS)
                            dve.wait_ge(b_gates_ready, L * 2 + i + 1)
                            g = p1[:, :, bass.ds(GATE_B + i * COLS, COLS)]
                            nc.vector.tensor_tensor(g, g, p1[:, :, bass.ds(BQ + i * B_HALF, COLS)], ALU.mult).then_inc(b_gated, 1)
                        if r == 11:
                            add_mod(H)
                            dve.wait_ge(squares_ready, L * A_HEADS + h + 1)
                            nc.vector.tensor_scalar(ms[:, 0:2], ss[:, 0:2], 1.0 / HD, EPS, ALU.mult, ALU.add).then_inc(ms_ready, 1)
                        if r == 11:
                            dve.wait_ge(rstd_ready, L * 6 + h + 1)
                            for t in range(TT):
                                ins = nc.vector.scalar_tensor_tensor(p1[:, t, bass.ds(AQ + h * HD, HD)], ps[7][:, t * HD:(t + 1) * HD], rstd[:, t:t + 1],
                                                                     vec["head_gain"][:, bass.ds(L * HD, HD)], ALU.mult, ALU.mult)
                            ins.then_inc(head_done, 1)
                dve.wait_ge(conv_turned, L + 1)
                for t in range(TT):
                    ins = nc.vector.bn_stats(stats[:, t, 0:6], ps[4 + t][:, :])
                ch.link(ins)
                dve.wait_ge(gates_ready, L + 1)
                nc.vector.tensor_tensor(p1[:, :, GATE_A:GATE_C], p1[:, :, GATE_A:GATE_C], p1[:, :, AQ:AQ + D_A], ALU.mult).then_inc(a_gated, 1)
                for t in range(TT):
                    ins = nc.vector.bn_aggr(mv[:, t, :], stats[:, t, 0:6])
                ch.link(ins)
                nc.vector.tensor_scalar(ms[:, 0:2], mv[:, 0:2, 1], EPS, None, ALU.add).then_inc(ms_ready, 1)
                dve.wait_ge(rstd_ready, L * 6 + 5)
                for t in range(TT):
                    ins = nc.vector.tensor_scalar(p1[:, t, AK:AK + D_C], ps[4 + t][:, :], mv[:, t, 0:1], rstd[:, t:t + 1], ALU.subtract, ALU.mult)
                ins.then_inc(cn_ready, 1)
                turn(8 + 16 * L, range(0, 6), Y_BANKS)
                dve.wait_ge(cpw_ready, L + 1)
                for t in range(TT):
                    ins = nc.vector.tensor_tensor(p1[:, t, GATE_C:W1], ps[t][:, :], p1[:, t, GATE_C:W1], ALU.mult)
                ins.then_inc(y_ready, 1)
                turn(8 + 16 * L, range(6, 8), Y_BANKS)
                for n in range(4):
                    for s in range(8):
                        if s == 7:
                            dve.wait_ge(chunk_used, 4 * B0 + 4 * AT_OUT + 8 * n + 8)
                            for t in range(TT):
                                xs = x[:, t, n * COLS:(n + 1) * COLS]
                                ins = nc.vector.scalar_tensor_tensor(xs, xs, ALPHA, ps[2 * (n % 2) + t][:, :], ALU.mult, ALU.add)
                            ins.then_inc(x_summed, 1)
                            dve.wait_ge(x_summed, L * 4 + n + 3)
                            for t in range(TT):
                                ins = nc.vector.bn_stats(stats[:, t, n * 6:(n + 1) * 6], x[:, t, n * COLS:(n + 1) * COLS])
                            if n == 3:
                                break
                        split(B0 + AT_OUT + 2 * n, s)
                        if n >= 2 and s == 2:
                            dve.wait_ge(ctx_landed, 16 * (L + 1))
                            for k in range(4):
                                c = nc.vector.bn_stats(stats[:, n, k * 6:(k + 1) * 6], ctx_tok[:, n - 2, k * COLS:(k + 1) * COLS])
                            if n == 3:
                                ch.link(c)
                        if n == 3 and s == 3:
                            for t in range(TT):
                                c = nc.vector.bn_aggr(mv[:, 2 + t, :], stats[:, 2 + t, :].rearrange("p (n s) -> p n s", s=6))
                            ch.link(c)
                        if n == 3 and s == 4:
                            ch.link(nc.vector.tensor_tensor(ms[:, 2:4], mv[:, 2:4, 0], mv[:, 2:4, 0], ALU.mult))
                ch.link(ins)
                nc.vector.scalar_tensor_tensor(ms[:, 2:4], ms[:, 2:4], RMS_EPS, mv[:, 2:4, 1], ALU.add, ALU.add)
                for t in range(TT):
                    ins = nc.vector.bn_aggr(mv[:, t, :], stats[:, t, :].rearrange("p (n s) -> p n s", s=6))
                ch.link(ins)
                nc.vector.tensor_scalar(ms[:, 0:2], mv[:, 0:2, 1], EPS, None, ALU.add).then_inc(ms_ready, 1)
                dve.wait_ge(rstd_ready, L * 6 + 6)
                dve.wait_ge(ln_landed, 32 * (L + 1))
                for n in range(4):
                    cols = slice(n * COLS, (n + 1) * COLS)
                    gain, shift = (ln_rows[k][:, n // 2, (n % 2) * COLS:(n % 2 + 1) * COLS] for k in range(2))
                    for t in range(TT):
                        ins = nc.vector.scalar_tensor_tensor(x[:, t, cols], x[:, t, cols], mv[:, t, 0:1], gain, ALU.subtract, ALU.mult)
                    ch.link(ins)
                    for t in range(TT):
                        ins = nc.vector.scalar_tensor_tensor(x[:, t, cols], x[:, t, cols], rstd[:, t:t + 1], shift, ALU.mult, ALU.add)
                    ins.then_inc(x_ready, 1)
                    if n:
                        turn(16 + 16 * L, range(2 * n - 2, 2 * n))
                turn(16 + 16 * L, range(6, 8))
                split(B0 + AT_OUT + 6, 7)

            dve.wait_ge(mod_done, MOD_GROUPS)
            n1 = vec["norm1"].rearrange("p (k c) -> p k c", c=2)
            nc.vector.scalar_tensor_tensor(hs1[:, :, :], mod3[:, KT:2 * KT, :], 1.0, n1, ALU.add, ALU.mult).then_inc(scale_ready, 1)
            nc.vector.scalar_tensor_tensor(hs2[:, :], mod3[:, 4 * KT:5 * KT, 0], 1.0, vec["norm2"], ALU.add, ALU.mult).then_inc(scale_ready, 1)

            def row_stats(tiles):
                for i, src in tiles:
                    for n in range(4):
                        ins = nc.vector.bn_stats(stats[:, i, n * 6:(n + 1) * 6], src[:, n * COLS:(n + 1) * COLS])
                ch.link(ins)

            def mean_squares(tiles):
                for i in tiles:
                    ins = nc.vector.bn_aggr(mv[:, i, :], stats[:, i, :].rearrange("p (n s) -> p n s", s=6))
                ch.link(ins)
                n = len(tiles)
                ch.link(nc.vector.tensor_tensor(ms[:, 0:n], mv[:, 0:n, 0], mv[:, 0:n, 0], ALU.mult))
                nc.vector.scalar_tensor_tensor(ms[:, 0:n], ms[:, 0:n], RMS_EPS, mv[:, 0:n, 1], ALU.add, ALU.add).then_inc(ms_ready, 1)

            for t in range(TT):
                ins = nc.vector.tensor_scalar(ctx_tok[:, t, :], ctx_tok[:, t, :], rstd[:, 2 + t:3 + t], None, ALU.mult)
                ins.then_inc(ctx_ready, 1)
            window = na_mask.rearrange("p (o c) -> p o c", o=1).to_broadcast([P, 8, GRID_W])
            turn_modulated(TURN_KVC)
            row_stats([(t, x[:, t, :]) for t in range(TT)])
            mean_squares(range(TT))
            dve.wait_ge(rstd_ready, 13)
            for t in range(TT):
                ins = nc.vector.tensor_scalar(xn[:, t, :], x[:, t, :], rstd[:, t:t + 1], None, ALU.mult)
            ins.then_inc(xn_ready, 1)
            with dve.Fori(0, 2) as i:
                for p in range(2):
                    for s in range(8):
                        split(AT_KVC + 4 * i + 2 * p, s)
                    dve.wait_ge(chunk_used, 4 * AT_KVC + 16 * i + 8 * p + 8)
                    copy_group(2 * p + 1, kvc[:, 1, bass.ds((2 * i + p) * COLS, COLS)])
                for n in range(4):
                    dve.wait_ge(na_flipped, 4 * i + n + 1)
                    nc.vector.tensor_tensor(shared[:, bass.ds(i * 2048 + n * 512, 512)].rearrange("p (a c) -> p a c", c=GRID_W),
                                            ps[4 + n][:, :].rearrange("p (a c) -> p a c", c=GRID_W), window, ALU.add).then_inc(na_biased, 1)
            turn_modulated(TURN_H)
            with dve.Fori(0, 5) as i:
                for p in range(2):
                    for s in range(8):
                        split(AT_IN2 + 4 * i + 2 * p, s)
                    dve.wait_ge(chunk_used, 4 * AT_IN2 + 16 * i + 8 * p + 8)
                    copy_group(2 * p + 1, p2[:, 1, bass.ds((2 * i + p) * COLS, COLS)])
            for s in range(8):
                if s == 7:
                    dve.wait_ge(chunk_used, 4 * AT_IN2 + 88)
                    copy_group(1, p2[:, 1, FT:FT + COLS])
                split(AT_IN2 + 20, s)
                if s == 0:
                    dve.wait_ge(evac_a, 46)
                    dve.wait_ge(evac_d, 46)
                    nc.vector.tensor_tensor(p2[:, :, SV:SV + COLS], p2[:, :, SV:SV + COLS], p2[:, :, SC:SC + COLS], ALU.mult).then_inc(u_ready, 1)
                    nc.vector.memset(pool_u[:, :, 0:8], 0.0)
                    nc.vector.memset(pool_u[:, :, 264:272], 0.0).then_inc(cleared, 1)
                if 2 <= s < 6:
                    g = s - 2
                    if g == 0:
                        dve.wait_ge(pool_copied, 1)
                        dve.wait_ge(inv_landed, 16)
                    src = pool_u[:, g, :]
                    for k in range(g + 1):
                        half_w, lo, hi = 2 ** k // 2, 2 ** k, 273 - 2 ** k
                        dst = pool_s[k % 2]
                        a, b = (1, 0) if k == 0 else (half_w, -half_w)
                        ch.link(nc.vector.tensor_tensor(dst[:, lo:hi], src[:, lo - a:hi - a], src[:, lo - b:hi - b], ALU.add))
                        src = dst
                    ch.link(nc.vector.tensor_tensor(pool_p[:, g, :], src[:, 8:264], pool_p[:, g, :], ALU.mult))
                    ins = nc.vector.tensor_tensor(pool_p[:, g, :], pool_p[:, g, :], pool_u[:, g, 8:264], ALU.subtract)
                    if g == 3:
                        ins.then_inc(pool_ready, 1)
            dve.wait_ge(squares_ready, DEPTH * A_HEADS + 8)
            nc.vector.tensor_scalar(ms[:, :], ss[:, :], 1.0 / HD, RMS_EPS, ALU.mult, ALU.add).then_inc(ms_ready, 1)
            dve.wait_ge(u_copied, 1)
            v = gflat.rearrange("p (j t) -> p j t", j=4)
            w = vec["short_w"]
            for k in range(3):
                for j in range(4):
                    u = conv_pad[:, j, CONV - 2 + k:CONV - 2 + k + S]
                    if k == 0:
                        ins = nc.vector.tensor_scalar(v[:, j, :], u, w[:, 3 * j:3 * j + 1], None, ALU.mult)
                    else:
                        ins = nc.vector.scalar_tensor_tensor(v[:, j, :], u, w[:, 3 * j + k:3 * j + k + 1], v[:, j, :], ALU.mult, ALU.add)
                ch.link(ins)
            for k in range(2):
                if k:
                    ins.then_inc(u_used, 1)
                ins = nc.vector.tensor_tensor(v[:, 2 * k:2 * k + 2, :], v[:, 2 * k:2 * k + 2, :], ps[6 + k][:, :].rearrange("p (j t) -> p j t", j=2), ALU.mult)
            ch.link(ins)
            ch.link(nc.vector.tensor_copy(br_hi[:, :, :], v))
            rest_of(br_lo[:, :, :], v, br_hi[:, :, :]).then_inc(br_ready, 1)

            def diagonal(dst, r):
                for j in range(4):
                    at = (2, 5)[r // 4] * KT + (r % 4) * 4 + j
                    ins = nc.vector.tensor_scalar(dst[:, j * P:(j + 1) * P], ident, mod3[:, at, 0:1], None, ALU.mult)
                ins.then_inc(diag_ready, 1)

            for turn_of in range(3):
                if turn_of == 1:
                    dve.wait_ge(pool_scaled, 1)
                    ch.link(nc.vector.tensor_copy(br_hi[:, :, :], pool_v))
                    rest_of(br_lo[:, :, :], pool_v, br_hi[:, :, :]).then_inc(br_ready, 1)
                if turn_of == 1:
                    dve.wait_ge(br_ready, 2)
                    for r in range(2):
                        diagonal(early_diag[:, r, :], r)
                if turn_of == 2:
                    for r in range(2, 8):
                        if r >= 6:
                            dve.wait_ge(row_ready, r - 3)
                        diagonal(diag[:, (r - 2) % 4, :], r)
                    dve.wait_ge(ft_ready, 1)
                    f = [ps[4 + k][:, :].rearrange("p (j t) -> p j t", j=2) for k in range(2)]
                    for k in range(2):
                        ins = nc.vector.tensor_copy(br_hi[:, 2 * k:2 * k + 2, :], f[k])
                    ch.link(ins)
                    for k in range(2):
                        ins = rest_of(br_lo[:, 2 * k:2 * k + 2, :], f[k], br_hi[:, 2 * k:2 * k + 2, :])
                    ins.then_inc(br_ready, 1)
                with dve.Fori(0, 2) as i, ch.loop(i, 2, DVE_GATES[turn_of]):
                    for s in range(20):
                        n, r = 2 * i + s // 10, s % 10
                        g = 4 * turn_of + n
                        H = 24 + g
                        split(AT_GATES + 10 * turn_of + 5 * i, s)
                        if r == 9:
                            dve.wait_ge(sig_done, g + 2)
                            dve.wait_ge(chunk_used, 4 * AT_GATES + 40 * turn_of + 20 * i + s + 1)
                            for t in range(TT):
                                y = p2[:, t, bass.ds(Y2 + n * COLS, COLS)]
                                ins = nc.vector.tensor_tensor(y if turn_of == 0 else gtmp[:, t, :], gtmp[:, t, :], ps[2 + t][:, :], ALU.mult)
                            if turn_of:
                                ch.link(ins)
                                for t in range(TT):
                                    y = p2[:, t, bass.ds(Y2 + n * COLS, COLS)]
                                    ins = nc.vector.tensor_tensor(y, y, gtmp[:, t, :], ALU.add)
                            ins.then_inc(gate_added, 1)
                        if turn_of == 2:
                            continue
                        if r == 4:
                            dve.wait_ge(scores_ready, H + 1)
                            for t in range(TT):
                                nc.vector.scalar_tensor_tensor(probs[:, t * 512:t * 512 + 256], ps[6 + t][:, 0:256], HEAD_SCALE,
                                                               na_bias[:, t, bass.ds(g * 256, 256)], ALU.mult, ALU.add)
                                ins = nc.vector.tensor_scalar(probs[:, t * 512 + 256:t * 512 + 512], ps[6 + t][:, 256:512], HEAD_SCALE, None, ALU.mult)
                            ch.link(ins)
                            row_maxima([(0, 512), (512, 1024)])
                        if r == 6:
                            dve.wait_ge(exps_ready, H + 1)
                            ch.link(nc.vector.reciprocal(recip[:, 0:2], sums[:, 0:2]))
                        if r == 8:
                            dve.wait_ge(pv_ready, H + 1)
                            for t in range(TT):
                                ins = nc.vector.tensor_scalar(p2[:, t, bass.ds(NQ + g * HD, HD)], ps[6][:, t * HD:(t + 1) * HD],
                                                              recip[:, t:t + 1], None, ALU.mult)
                            ins.then_inc(head_done, 1)
            with dve.Fori(0, 2) as i:
                for p in range(2):
                    for s in range(8):
                        split(AT_GATE0 + 4 * i + 2 * p, s)
            turn(TURN_NA, range(4))
            with dve.Fori(0, 2) as i, ch.loop(i, 2, 2):
                for s in range(8):
                    p = s // 4
                    if s % 4 == 3:
                        dve.wait_ge(sig_done, 17)
                        dve.wait_ge(chunk_used, 4 * AT_NAP + 8 * i + s + 1)
                        dve.wait_ge(gate_added, 13 + 2 * i + p)
                        for t in range(TT):
                            ins = nc.vector.tensor_tensor(gtmp[:, t, :], kvc[:, t, bass.ds((2 * i + p) * COLS, COLS)], ps[2 * p + t][:, :], ALU.mult)
                        ch.link(ins)
                        for t in range(TT):
                            y = p2[:, t, bass.ds(Y2 + (2 * i + p) * COLS, COLS)]
                            ins = nc.vector.tensor_tensor(y, y, gtmp[:, t, :], ALU.add)
                        ins.then_inc(gate_added, 1)
                    split(AT_NAP + 2 * i, s)
            turn(TURN_Y2)
            ch.link(nc.vector.memset(p2[:, :, Y2:Y2 + D], 0.0))
            for n in range(4):
                for s in range(8):
                    if s == 7:
                        dve.wait_ge(chunk_used, 4 * AT_WO + 8 * n + 8)
                        dve.wait_ge(x_summed, 2 + 4 * DEPTH + n)
                        dve.wait_ge(row_copied, 8)
                        g1 = p2[:, n // 2, NV + (n % 2) * COLS:NV + (n % 2 + 1) * COLS]
                        for t in range(TT):
                            ins = nc.vector.tensor_tensor(gtmp[:, t, :], ps[2 * (n % 2) + t][:, :], g1, ALU.mult)
                        ch.link(ins)
                        for t in range(TT):
                            xs = x[:, t, n * COLS:(n + 1) * COLS]
                            ins = nc.vector.tensor_tensor(xs, xs, gtmp[:, t, :], ALU.add)
                        ins.then_inc(x_summed, 1)
                        dve.wait_ge(x_summed, 2 + 4 * DEPTH + n + 1)
                        for t in range(TT):
                            ins = nc.vector.bn_stats(stats[:, t, n * 6:(n + 1) * 6], x[:, t, n * COLS:(n + 1) * COLS])
                        ch.link(ins)
                        if n == 3:
                            break
                    split(AT_WO + 2 * n, s)
            mean_squares(range(TT))
            dve.wait_ge(rstd_ready, 15)
            for n in range(4):
                for t in range(TT):
                    cols = slice(n * COLS, (n + 1) * COLS)
                    ins = nc.vector.tensor_scalar(kvc[:, t, cols], x[:, t, cols], rstd[:, t:t + 1], None, ALU.mult)
                ins.then_inc(h2_ready, 1)
            turn_modulated(TURN_H2)
            split(AT_WO + 6, 7)

            def hidden(f):
                dve.wait_ge(silu_done, f + 1)
                for t in range(TT):
                    ins = nc.vector.tensor_tensor(kvc[:, t, 0:COLS], gtmp[:, t, :], ps[2 + t][:, :], ALU.mult)
                ins.then_inc(hid_ready, 1)

            def hidden_lo(f):
                dve.wait_ge(hid_hi, f + 1)
                for k in range(2):
                    ins = rest_of(br_lo[:, 2 * k:2 * k + 2, :], ps[4 + k][:, :].rearrange("p (j t) -> p j t", j=2), br_hi[:, 2 * k:2 * k + 2, :])
                ins.then_inc(hid_lo, 1)

            for s in range(16):
                split(AT_FF, s)
            dve.wait_ge(chunk_used, 4 * AT_FF + 16)
            hidden(0)
            with dve.Fori(0, FF - 1) as i:
                for s in range(24):
                    split(AT_FF + 4 + 6 * i, s)
                    if s == 7:
                        hidden_lo(i)
                    if s == 15:
                        dve.wait_ge(chunk_used, 4 * AT_FF + 16 + 24 * i + 16)
                        hidden(i + 1)
                    if s >= 16 and s % 2:
                        dve.wait_ge(chunk_used, 4 * AT_FF + 16 + 24 * i + s + 1)
                        dve.wait_ge(acc_done, 2)
                        for t in range(TT):
                            n = (s - 16) // 2
                            acc = p2[:, t, Y2 + n * COLS:Y2 + (n + 1) * COLS]
                            ins = nc.vector.tensor_tensor(acc, acc, ps[((4, 5) if n % 2 else (6, 7))[t]][:, :], ALU.add)
                        ins.then_inc(acc_done, 1)
            hidden_lo(FF - 1)
            for s in range(8):
                if s < 4:
                    split(BARS - 2, s)
                if s % 2:
                    n = s // 2
                    cols = slice(Y2 + n * COLS, Y2 + (n + 1) * COLS)
                    g2 = p2[:, n // 2, NK + (n % 2) * COLS:NK + (n % 2 + 1) * COLS]
                    dve.wait_ge(chunk_used, 4 * BARS - 8 + s + 1)
                    for t in range(TT):
                        ins = nc.vector.tensor_tensor(p2[:, t, cols], p2[:, t, cols], ps[((4, 5) if n % 2 else (6, 7))[t]][:, :], ALU.add)
                    ins.then_inc(acc_done, 1)
                    dve.wait_ge(acc_done, 4 * (FF - 1) + n + 3)
                    for t in range(TT):
                        ins = nc.vector.tensor_tensor(p2[:, t, cols], p2[:, t, cols], g2, ALU.mult)
                    ch.link(ins)
                    for t in range(TT):
                        xs = x[:, t, n * COLS:(n + 1) * COLS]
                        ins = nc.vector.tensor_tensor(xs, xs, p2[:, t, cols], ALU.add)
                    ins.then_inc(out_ready, 1)


def position_bucket(d):
    exact = N_BUCKETS // 2
    df = np.maximum(d, 1).astype(np.float32)
    large = exact + (np.log(df / np.float32(exact)) / np.float32(math.log(MAX_DISTANCE / exact)) * np.float32(N_BUCKETS - exact)).astype(np.int32)
    return np.where(d < exact, d, np.minimum(large, N_BUCKETS - 1))


def shape_constants():
    consts = np.zeros((P + N_BUCKETS + A_HEADS + B_HEADS, 384), np.float32)
    consts[0:P, 0:128] = np.eye(P)
    consts[0:P, 128:256] = np.eye(P)[::-1]
    j, c = np.arange(P) % GRID_W, np.arange(GRID_W)
    first = np.clip(j - NA_KW // 2, 0, GRID_W - NA_KW)[:, None]
    consts[0:P, 256:320] = np.where((c >= first) & (c < first + NA_KW), 0.0, MASKED)
    consts[[0, 1, 2, 3], [320, 321, 320, 321]] = 1.0
    d = S - 1 - np.arange(384)
    seen = d >= 0
    consts[P + position_bucket(np.maximum(d, 0))[seen], np.arange(384)[seen]] = 1.0
    times = seen * ((d <= 128).astype(int) + (d % 4 == 0) + (d % 16 == 0))
    at = P + N_BUCKETS
    consts[at:at + A_HEADS] = np.where(seen, 0.0, MASKED)
    consts[at + A_HEADS:at + A_HEADS + B_HEADS] = np.where(times > 0, np.log(np.maximum(times, 1)), MASKED)
    pos, ch = np.outer(np.arange(S), np.arange(S)) * (2 * np.pi / S), np.outer(np.arange(P), np.arange(P)) * (2 * np.pi / P)
    norm = 1.0 / math.sqrt(S * P)
    rows = np.concatenate([np.cos(pos), np.sin(pos)], axis=1).reshape(TT, P, 2 * S)
    dft = np.concatenate([rows[0], rows[1], np.cos(ch) * norm, -np.sin(ch) * norm], axis=1).astype(np.float32)
    t = np.arange(S)
    inv = np.stack([1.0 / (np.clip(t - w // 2 + w, 0, S) - np.clip(t - w // 2, 0, S)) for w in POOL_WINDOWS])
    inv = np.broadcast_to(inv.astype(np.float32), (P, 4, S))
    return consts, np.ascontiguousarray(dft), np.ascontiguousarray(inv)


def weight_stream(a):
    stream = np.empty((BARS, P, TILES_PER_BAR, COLS), np.float32)
    at = 0

    def put(w, row, col):
        nonlocal at
        stream[at // TILES_PER_BAR, :, at % TILES_PER_BAR, :] = w[row * P:(row + 1) * P, col * COLS:(col + 1) * COLS]
        at += 1

    def put_group(w, col, k0=0, k1=None):
        for k in range(k0, w.shape[0] // P if k1 is None else k1):
            put(w, k, col)

    w_mod = a["w_mod_2"][0]
    order = [12, 13, 4, 6, 8, 5, 7, 9, 0, 1, 2, 10, 11, 3, 14]
    mixed = [*range(4, 12), *range(0, 4), *range(12, 16)]
    for layer in range(DEPTH):
        w = a["w_in"][layer]
        for g in order[:5]:
            put_group(w, g)
        for h in range(B_HEADS):
            for part, k in MIX:
                put_group(*((w, order[5 + h]) if part == "group" else (w_mod, layer * 12 + h)), 2 * k, 2 * k + 2)
        for h in range(A_HEADS):
            for r in range(4):
                put_group(w_mod, layer * 12 + B_HEADS + h, 4 * r, 4 * r + 4)
                k = 2 * (4 * (h % 2) + r)
                put_group(w, order[13 + h // 2], k, k + 2)
        for g in range(D // COLS):
            for k in mixed:
                put(a["w_out"][layer], k, g)
    w = a["w_in_2"][0]
    for g in (2, 3, 4, 5):
        put_group(w, g)
    for g in (0, 1, 2, 3, 4, 5, 7, 8, 9, 10, 6):
        put_group(w, g)
    gates = a["w_gate_2"][0]
    for i, branch in ((3, "w_pd_2"), (2, "w_pc_2"), (1, "w_pb_2")):
        for g in range(D // COLS):
            put_group(gates[i], g)
            put_group(a[branch][0], g)
    for w in (gates[0], a["w_pa_2"][0], a["w_o_2"][0]):
        for g in range(D // COLS):
            put_group(w, g)
    w_gate, w_up, w_down = (a[f"w_ffn_{n}_2"][0] for n in ("gate", "up", "down"))
    for f in range(FF + 1):
        if f < FF:
            put_group(w_gate, f)
            put_group(w_up, f)
        if f:
            for g in range(D // COLS):
                put_group(w_down, g, 4 * (f - 1), 4 * f)
    assert at == BARS * TILES_PER_BAR
    return stream.reshape(BARS, P, TILES_PER_BAR * COLS)


def columns(v, n):
    return v.reshape(n, P).T


def parameter_vectors(a):
    twice = lambda v: np.repeat(v[:, :, None], 2, axis=2).reshape(P, -1)
    per_layer = lambda v: np.concatenate([columns(v[layer], 4) for layer in range(DEPTH)], axis=1)
    rel = np.zeros((P, A_HEADS + B_HEADS), np.float32)
    rel[0:N_BUCKETS] = a["rel_bias"]
    dw = a["conv_dw"].reshape(DEPTH, CONV, 4, P).transpose(3, 0, 2, 1).reshape(P, -1)
    parts = {
        "c_cols": np.stack([columns(a["c_2"][0], KT), columns(a["c_ctx_2"], KT)], axis=2).reshape(P, -1),
        "b_mod": twice(columns(a["b_mod_2"][0], N_MOD * KT)),
        "rel_bias": rel,
        "head_gain": np.broadcast_to(a["diff_head_gain"].reshape(1, -1), (P, DEPTH * HD)),
        "conv_dw": dw,
        "conv_b": per_layer(a["conv_b"]), "conv_g": per_layer(a["conv_ln_g"]), "conv_beta": per_layer(a["conv_ln_b"]),
        "norm1": twice(columns(a["norm1_w_2"][0], KT)),
        "norm2": columns(a["norm2_w_2"][0], KT),
        "q_norm": a["q_norm_w_2"].reshape(P, 1), "k_norm": a["k_norm_w_2"].reshape(P, 1),
        "pool_scale": columns(a["pool_scale_2"][0], 4),
        "short_w": a["conv_w_2"][0].reshape(3, 4, P).transpose(2, 1, 0).reshape(P, -1),
    }
    assert all(parts[n].shape == (P, w) for n, w in VECS), [(n, parts[n].shape) for n, _ in VECS]
    return np.ascontiguousarray(np.concatenate([parts[n] for n, _ in VECS], axis=1))


def kernel(**inputs):
    import concourse.bacc as bacc
    from concourse.bass_utils import run_bass_kernel_spmd

    a = {k: np.asarray(v) for k, v in inputs.items()}
    consts, dft, inv = shape_constants()
    arrays = {
        "weights": weight_stream(a),
        "x_in": np.ascontiguousarray(a["x"].reshape(S, D)),
        "consts": consts,
        "vecs": parameter_vectors(a),
        "lam_rows": np.ascontiguousarray(a["diff_lambda"].reshape(1, -1)),
        "rpb": np.ascontiguousarray(a["rpb_2"].reshape(NA_HEADS, RPB_H * RPB_W)),
        "ctx_in": np.ascontiguousarray(a["ctx_2"].reshape(S, D)),
        "ln_gb": np.ascontiguousarray(np.stack([a["ln_g"], a["ln_b"]], axis=1)),
        "conv_pw": np.ascontiguousarray(a["conv_pw"].reshape(DEPTH * 4, P, COLS)),
        "cs_dft": dft,
        "inv_cnt": inv,
        "w_pool": np.ascontiguousarray(a["w_pool_2"][0].transpose(1, 0, 2).reshape(P, 4 * P)),
    }
    nc = bacc.Bacc("TRN2", target_bir_lowering=False, num_devices=1)
    args = [nc.dram_tensor(n, v.shape, F32, kind="ExternalInput").ap() for n, v in arrays.items()]
    scratch = nc.dram_tensor("scratch", (A_HEADS + B_HEADS, 384), F32, kind="Internal").ap()
    out = nc.dram_tensor("out", (S, D), F32, kind="ExternalOutput").ap()
    build(nc, *args, scratch, out)
    r = run_bass_kernel_spmd(nc, [arrays], core_ids=[0])
    return r.results[0]["out"].reshape(1, S, D)
```
